# Optimizing a Trainium2 kernel written in Bass

```python
import math
import jax, jax.numpy as jnp
from jax import lax
import numpy as np

D_MODEL = 2048
BATCH = 1
SEQ = 256
DEPTH = 1

HEAD_DIM = 128
DIL_GROUPS = ((128, 1), (512, 4), (2048, 16))
HEADS_PER_DIL_GROUP = 4
N_HEADS_A = HEADS_PER_DIL_GROUP * len(DIL_GROUPS)
N_HEADS_B = 4
WIDTH_A = N_HEADS_A * HEAD_DIM
WIDTH_B = N_HEADS_B * HEAD_DIM
A_OUT = HEADS_PER_DIL_GROUP * HEAD_DIM
D_IN = 3 * WIDTH_A + 3 * WIDTH_B + 2 * D_MODEL
D_FF = 5632
CONV_WIDTH = 3
PLE_DIM = 256
BLOCK = 128
RMS_EPS = 1e-6
ALIBI_MAX = 8.0


def rmsnorm(x, g):
    xf = x.astype(jnp.float32)
    y = xf * lax.rsqrt(jnp.mean(xf * xf, axis=-1, keepdims=True) + RMS_EPS)
    return (y * g.astype(jnp.float32)).astype(x.dtype)

def alibi_slopes(n):
    return jnp.exp2(-ALIBI_MAX * jnp.arange(1, n + 1, dtype=jnp.float32) / n)

def dilated_window_group(q, k, v, window, dilation, slopes):
    b, s, hg, dh = q.shape
    n_back = window // dilation
    span = dilation * BLOCK
    s_pad = -(-s // span) * span
    L = s_pad // dilation
    nb = L // BLOCK

    def to_blocks(t):
        t = jnp.pad(t, ((0, 0), (0, s_pad - s), (0, 0), (0, 0)))
        t = t.reshape(b, L, dilation, hg, dh).transpose(0, 2, 3, 1, 4)
        return t.reshape(b, dilation, hg, nb, BLOCK, dh)

    def with_prev(t):
        prev = jnp.pad(t, ((0, 0), (0, 0), (0, 0), (1, 0), (0, 0), (0, 0)))[:, :, :, :-1]
        return jnp.concatenate([prev, t], axis=4)

    qb = to_blocks(q)
    kk = with_prev(to_blocks(k))
    vv = with_prev(to_blocks(v))
    scores = jnp.einsum('brhnqe,brhnke->brhnqk', qb, kk).astype(jnp.float32) * (1.0 / math.sqrt(dh))
    qi = jnp.arange(BLOCK)[:, None]
    ki = jnp.arange(2 * BLOCK)[None, :]
    steps = BLOCK + qi - ki
    valid = (steps >= 0) & (steps <= n_back)
    first = (jnp.arange(nb) == 0)[:, None, None]
    valid = valid[None] & ~(first & (ki < BLOCK)[None])
    bias = -slopes[:, None, None] * (steps * dilation).astype(jnp.float32)[None]
    scores = scores + bias[None, None, :, None]
    scores = jnp.where(valid[None, None, None], scores, -jnp.inf)
    lse = jax.nn.logsumexp(scores, axis=-1)
    probs = jnp.exp(scores - lse[..., None])
    out = jnp.einsum('brhnqk,brhnke->brhnqe', probs.astype(v.dtype), vv)

    def from_blocks(t):
        t = t.reshape(b, dilation, hg, L, *t.shape[5:])
        t = jnp.moveaxis(t, 3, 1)
        return t.reshape(b, s_pad, hg, *t.shape[4:])[:, :s]

    return from_blocks(out), from_blocks(lse)

def dilated_mixture_attention(q, k, v):
    b, s = q.shape[:2]
    slopes = alibi_slopes(N_HEADS_A)
    outs, lses = [], []
    for g, (window, dilation) in enumerate(DIL_GROUPS):
        sl = slice(g * HEADS_PER_DIL_GROUP, (g + 1) * HEADS_PER_DIL_GROUP)
        o, l = dilated_window_group(q[:, :, sl], k[:, :, sl], v[:, :, sl], window, dilation, slopes[sl])
        outs.append(o)
        lses.append(l)
    alpha = jax.nn.softmax(jnp.stack(lses), axis=0)
    y = jnp.sum(alpha[..., None] * jnp.stack(outs).astype(jnp.float32), axis=0)
    return y.reshape(b, s, A_OUT).astype(q.dtype)

def stick_breaking_attention(q, k, v):
    b, s, h, dh = q.shape
    nb = s // BLOCK
    qt = q.transpose(0, 2, 1, 3)
    kt = k.transpose(0, 2, 1, 3)
    vt = v.transpose(0, 2, 1, 3)
    scale = 1.0 / math.sqrt(dh)
    idx = jnp.arange(BLOCK)
    tri_within = (idx[:, None] > idx[None, :]).astype(jnp.float32)
    diag_before = idx[None, :] < idx[:, None]
    outs = []
    for n in range(nb):
        c = n + 1
        kl = c * BLOCK
        qblk = qt[:, :, n * BLOCK:(n + 1) * BLOCK]
        z = jnp.einsum('bhqe,bhke->bhqk', qblk, kt[:, :, :kl]).astype(jnp.float32) * scale
        before = jnp.concatenate([jnp.ones((BLOCK, n * BLOCK), dtype=bool), diag_before], axis=1)
        ln = jnp.where(before, jax.nn.log_sigmoid(-z), 0.0)
        lnc = ln.reshape(b, h, BLOCK, c, BLOCK)
        within = jnp.einsum('bhqcj,ji->bhqci', lnc, tri_within)
        tot = jnp.sum(lnc, axis=-1)
        cidx = jnp.arange(c)
        after = jnp.einsum('bhqc,cd->bhqd', tot, (cidx[:, None] > cidx[None, :]).astype(jnp.float32))
        logw = z.reshape(b, h, BLOCK, c, BLOCK) + lnc + within + after[..., None]
        w = jnp.where(before, jnp.exp(logw.reshape(b, h, BLOCK, kl)), 0.0)
        outs.append(jnp.einsum('bhqk,bhke->bhqe', w.astype(v.dtype), vt[:, :, :kl]))
    out = jnp.concatenate(outs, axis=2)
    return out.transpose(0, 2, 1, 3).reshape(b, s, h * dh)

def causal_depthwise_conv(x, w, bias):
    s = x.shape[1]
    xp = jnp.pad(x, ((0, 0), (CONV_WIDTH - 1, 0), (0, 0)))
    y = bias + w[0] * xp[:, 0:s]
    for j in range(1, CONV_WIDTH):
        y = y + w[j] * xp[:, j:j + s]
    return y

def first_inputs(seed: int = 0) -> dict:
    key = jax.random.key(seed)
    ks = jax.random.split(key, 20)
    f32 = jnp.float32

    def nrm(k, shape, scale):
        return jax.random.normal(k, shape, f32) * scale

    def gain(k):
        return 1.0 + 0.05 * jax.random.normal(k, (DEPTH, D_MODEL), f32)

    return {
        'x': nrm(ks[0], (BATCH, SEQ, D_MODEL), 1.0),
        'p': nrm(ks[1], (DEPTH, BATCH, SEQ, PLE_DIM), 1.0),
        'g_mix_pre': gain(ks[2]),
        'w_in': nrm(ks[3], (DEPTH, D_MODEL, D_IN), D_MODEL ** -0.5),
        'w_branch_a': nrm(ks[4], (DEPTH, A_OUT, D_MODEL), A_OUT ** -0.5),
        'w_branch_b': nrm(ks[5], (DEPTH, WIDTH_B, D_MODEL), WIDTH_B ** -0.5),
        'w_out': nrm(ks[6], (DEPTH, D_MODEL, D_MODEL), D_MODEL ** -0.5),
        'g_mix_post': gain(ks[7]),
        'g_ffn_pre': gain(ks[8]),
        'w_up': nrm(ks[9], (DEPTH, D_MODEL, 2 * D_FF), D_MODEL ** -0.5),
        'conv_w': nrm(ks[10], (DEPTH, CONV_WIDTH, 2 * D_FF), CONV_WIDTH ** -0.5),
        'conv_b': nrm(ks[11], (DEPTH, 2 * D_FF), 0.01),
        'w_down': nrm(ks[12], (DEPTH, D_FF, D_MODEL), D_FF ** -0.5),
        'g_ffn_post': gain(ks[13]),
        'w_ple_in': nrm(ks[14], (DEPTH, PLE_DIM, D_MODEL), PLE_DIM ** -0.5),
        'w_ple_gate': nrm(ks[15], (DEPTH, D_MODEL, D_MODEL), D_MODEL ** -0.5),
    }

def first_block(x, p, g_mix_pre, w_in, w_branch_a, w_branch_b, w_out, g_mix_post, g_ffn_pre, w_up, conv_w, conv_b, w_down, g_ffn_post, w_ple_in, w_ple_gate):
    b, s, _ = x.shape
    splits = [WIDTH_A, 2 * WIDTH_A, 3 * WIDTH_A,
              3 * WIDTH_A + WIDTH_B, 3 * WIDTH_A + 2 * WIDTH_B, 3 * WIDTH_A + 3 * WIDTH_B,
              3 * WIDTH_A + 3 * WIDTH_B + D_MODEL]
    h = x
    for i in range(DEPTH):
        u = rmsnorm(h, g_mix_pre[i])
        proj = u @ w_in[i]
        qa, ka, va, qb, kb, vb, gla, glb = jnp.split(proj, splits, axis=-1)
        heads_a = lambda t: t.reshape(b, s, N_HEADS_A, HEAD_DIM)
        heads_b = lambda t: t.reshape(b, s, N_HEADS_B, HEAD_DIM)
        ya = dilated_mixture_attention(heads_a(qa), heads_a(ka), heads_a(va)) @ w_branch_a[i]
        yb = stick_breaking_attention(heads_b(qb), heads_b(kb), heads_b(vb)) @ w_branch_b[i]
        gate_a = jax.nn.sigmoid(gla.astype(jnp.float32)).astype(h.dtype)
        gate_b = jax.nn.sigmoid(glb.astype(jnp.float32)).astype(h.dtype)
        mix = (gate_a * ya + gate_b * yb) @ w_out[i]
        h = h + rmsnorm(mix, g_mix_post[i])
        u = rmsnorm(h, g_ffn_pre[i])
        up = causal_depthwise_conv(u @ w_up[i], conv_w[i], conv_b[i])
        gate_ff, value = jnp.split(up, [D_FF], axis=-1)
        f = (jax.nn.gelu(gate_ff, approximate=True) * value) @ w_down[i]
        h = h + rmsnorm(f, g_ffn_post[i])
        e = p[i] @ w_ple_in[i]
        h = h + jax.nn.sigmoid((h @ w_ple_gate[i]).astype(jnp.float32)).astype(h.dtype) * e
    return h


DEPTH_2 = 2

CTX_LEN = 256
GRID_W = 64
EPS = 1e-6

POOL_WINDOWS = (2, 4, 8, 16)
POOL_W = D_MODEL // 2
POOL_GROUP = POOL_W // len(POOL_WINDOWS)
CONV_W = D_MODEL // 2
CONV_K = 3
EVEN_IN = 2 * POOL_W + 4 * CONV_W

HG_DK = 128
HG_HEADS = D_MODEL // HG_DK
HG_DV = D_MODEL // HG_HEADS
HG_K = HG_HEADS * HG_DK
HG_V = HG_HEADS * HG_DV
ODD_IN = 3 * HG_K + 2 * HG_V
CHUNK = 64

N_EVEN = (DEPTH_2 + 1) // 2
N_ODD = DEPTH_2 // 2


def rms_norm(x, g):
    xf = x.astype(jnp.float32)
    y = xf * lax.rsqrt(jnp.mean(xf * xf, axis=-1, keepdims=True) + EPS)
    return (y * g.astype(jnp.float32)).astype(x.dtype)

def box_mean(x, w, axis):
    n = x.shape[axis]
    cs = jnp.cumsum(x.astype(jnp.float32), axis=axis)
    pad = [(0, 0)] * x.ndim
    pad[axis] = (1, 0)
    cs = jnp.pad(cs, pad)
    t = jnp.arange(n)
    lo = jnp.maximum(t - w // 2, 0)
    hi = jnp.minimum(t + w // 2 - 1, n - 1)
    s = jnp.take(cs, hi + 1, axis=axis) - jnp.take(cs, lo, axis=axis)
    cnt = (hi - lo + 1).astype(jnp.float32).reshape((n,) + (1,) * (x.ndim - axis - 1))
    return (s / cnt).astype(x.dtype)

def multiscale_pool(v, pool_w, pool_scale, on_grid):
    b, n, _ = v.shape
    outs = []
    for gi, w in enumerate(POOL_WINDOWS):
        vg = v[..., gi * POOL_GROUP:(gi + 1) * POOL_GROUP]
        if on_grid:
            rows = n // GRID_W
            m = box_mean(box_mean(vg.reshape(b, rows, GRID_W, POOL_GROUP), w, 1), w, 2)
            m = m.reshape(b, n, POOL_GROUP)
        else:
            m = box_mean(vg, w, 1)
        outs.append(m - vg)
    pooled = jnp.stack(outs, axis=2)
    mixed = jnp.einsum('bngi,gio->bngo', pooled, pool_w).reshape(b, n, POOL_W)
    return mixed * pool_scale

def depthwise_conv3(u, w, bias):
    n = u.shape[1]
    up = jnp.pad(u, ((0, 0), (1, 1), (0, 0)))
    return up[:, :n] * w[0] + up[:, 1:n + 1] * w[1] + up[:, 2:] * w[2] + bias

def pool_conv_mixer(h, w_in, pool_w, pool_scale, conv_w, conv_b, w_out, on_grid):
    idx = [int(i) for i in np.cumsum([POOL_W, POOL_W, CONV_W, CONV_W, CONV_W])]
    a_v, a_g, b_x, b_b, b_c, b_g = jnp.split(h @ w_in, idx, axis=-1)
    a_out = multiscale_pool(a_v, pool_w, pool_scale, on_grid) * jax.nn.silu(a_g)
    b_out = b_b * depthwise_conv3(b_c * b_x, conv_w, conv_b) * jax.nn.silu(b_g)
    return jnp.concatenate([a_out, b_out], axis=-1) @ w_out

def _heads(t, d):
    return t.reshape(t.shape[0], t.shape[1], HG_HEADS, d)

def _chunks(t):
    b, n, hh, d = t.shape
    return t.reshape(b, n // CHUNK, CHUNK, hh, d)

def _rev(t, reverse):
    return jnp.flip(t, axis=1) if reverse else t

def hgrn2_gates(z, lb):
    zf = z.astype(jnp.float32)
    f = lb + (1.0 - lb) * jax.nn.sigmoid(zf)
    k = (1.0 - lb) * jax.nn.sigmoid(-zf)
    return _heads(k, HG_DK), _heads(jnp.log(f), HG_DK)

def chunk_state_scan(kc, vc, bc, s0, keep_starts):
    b_last = bc[:, :, -1]
    k_dec = kc * jnp.exp(b_last[:, :, None] - bc)
    ds = jnp.einsum('bnchk,bnchv->bnhkv', k_dec, vc)
    decay = jnp.exp(b_last)

    def step(s, inp):
        d, dsn = inp
        return d[..., None] * s + dsn, (s if keep_starts else None)

    s_fin, starts = lax.scan(step, s0, (jnp.moveaxis(decay, 1, 0), jnp.moveaxis(ds, 1, 0)))
    return s_fin, starts

def hgrn2_chunk_scan(q, k, v, logf, s0):
    qc, kc, vc = _chunks(q), _chunks(k), _chunks(v)
    bc = jnp.cumsum(_chunks(logf), axis=2)
    s_fin, starts = chunk_state_scan(kc, vc, bc, s0, True)
    starts = jnp.moveaxis(starts, 0, 1)
    q_dec = qc * jnp.exp(bc)
    k_inv = kc * jnp.exp(-bc)
    inter = jnp.einsum('bnchk,bnhkv->bnchv', q_dec, starts)
    scores = jnp.einsum('bnchk,bnshk->bnhcs', q_dec, k_inv)
    mask = jnp.tril(jnp.ones((CHUNK, CHUNK), dtype=bool))
    scores = jnp.where(mask, scores, 0.0)
    intra = jnp.einsum('bnhcs,bnshv->bnchv', scores, vc)
    o = (inter + intra).reshape(q.shape[0], q.shape[1], HG_HEADS, HG_DV)
    return o, s_fin

def hgrn2_final_state(k, v, logf, s0):
    bc = jnp.cumsum(_chunks(logf), axis=2)
    s_fin, _ = chunk_state_scan(_chunks(k), _chunks(v), bc, s0, False)
    return s_fin

def hgrn2_readout(o, g, onorm_g, w_out):
    b, n = o.shape[:2]
    o = o * lax.rsqrt(jnp.mean(o * o, axis=-1, keepdims=True) + EPS)
    o = o.reshape(b, n, HG_V) * onorm_g.astype(jnp.float32) * jax.nn.silu(g.astype(jnp.float32))
    return o.astype(g.dtype) @ w_out

def hgrn2_mixer(h_lat, h_ctx, w_in, onorm_g, w_out, lb_fwd, lb_bwd, ctx_out):
    idx = [int(i) for i in np.cumsum([HG_K, HG_K, HG_V, HG_K])]
    zf_l, zb_l, i_l, q_l, g_l = jnp.split(h_lat @ w_in, idx, axis=-1)
    if ctx_out:
        zf_c, zb_c, i_c, q_c, g_c = jnp.split(h_ctx @ w_in, idx, axis=-1)
        q_c = _heads(q_c.astype(jnp.float32), HG_DK)
    else:
        zf_c, zb_c, i_c = jnp.split(h_ctx @ w_in[:, :idx[2]], idx[:2], axis=-1)
    q_l = _heads(q_l.astype(jnp.float32), HG_DK)
    v_l = _heads(i_l.astype(jnp.float32), HG_DV)
    v_c = _heads(i_c.astype(jnp.float32), HG_DV)
    s0 = jnp.zeros((h_lat.shape[0], HG_HEADS, HG_DK, HG_DV), jnp.float32)
    outs_l, outs_c = [], []
    for lb, z_l, z_c, reverse in ((lb_fwd, zf_l, zf_c, False), (lb_bwd, zb_l, zb_c, True)):
        k_l, lf_l = hgrn2_gates(z_l, lb)
        k_c, lf_c = hgrn2_gates(z_c, lb)
        if ctx_out:
            o_c, s_ctx = hgrn2_chunk_scan(_rev(q_c, reverse), _rev(k_c, reverse),
                                          _rev(v_c, reverse), _rev(lf_c, reverse), s0)
            outs_c.append(_rev(o_c, reverse))
        else:
            s_ctx = hgrn2_final_state(_rev(k_c, reverse), _rev(v_c, reverse),
                                      _rev(lf_c, reverse), s0)
        o_l, _ = hgrn2_chunk_scan(_rev(q_l, reverse), _rev(k_l, reverse),
                                  _rev(v_l, reverse), _rev(lf_l, reverse), s_ctx)
        outs_l.append(_rev(o_l, reverse))
    y_l = hgrn2_readout(outs_l[0] + outs_l[1], g_l, onorm_g, w_out)
    y_c = hgrn2_readout(outs_c[0] + outs_c[1], g_c, onorm_g, w_out) if ctx_out else None
    return y_l, y_c

def second_inputs(seed: int = 0) -> dict:
    key = jax.random.key(seed)
    ks = jax.random.split(key, 18)
    D = D_MODEL

    def nrm(k, shape, s):
        return jax.random.normal(k, shape, jnp.float32) * s

    return {
        "x": nrm(ks[0], (BATCH, SEQ, D), 1.0),
        "c": nrm(ks[1], (BATCH, D), 1.0),
        "ctx": nrm(ks[2], (BATCH, CTX_LEN, D), 1.0),
        "c_ctx": nrm(ks[3], (D,), 1.0),
        "ada_w": nrm(ks[4], (DEPTH_2, D, 3 * D), 0.5 * D ** -0.5),
        "ada_b": nrm(ks[5], (DEPTH_2, 3 * D), 0.01),
        "pre_g": 1.0 + nrm(ks[6], (DEPTH_2, D), 0.05),
        "post_g": 1.0 + nrm(ks[7], (DEPTH_2, D), 0.05),
        "ev_w_in": nrm(ks[8], (N_EVEN, D, EVEN_IN), D ** -0.5),
        "ev_pool_w": nrm(ks[9], (N_EVEN, len(POOL_WINDOWS), POOL_GROUP, POOL_GROUP), POOL_GROUP ** -0.5),
        "ev_pool_scale": 1.0 + nrm(ks[10], (N_EVEN, POOL_W), 0.1),
        "ev_conv_w": nrm(ks[11], (N_EVEN, CONV_K, CONV_W), CONV_K ** -0.5),
        "ev_conv_b": nrm(ks[12], (N_EVEN, CONV_W), 0.01),
        "ev_w_out": nrm(ks[13], (N_EVEN, POOL_W + CONV_W, D), (POOL_W + CONV_W) ** -0.5),
        "od_w_in": nrm(ks[14], (N_ODD, D, ODD_IN), D ** -0.5),
        "od_onorm_g": 1.0 + nrm(ks[15], (N_ODD, HG_V), 0.05),
        "od_w_out": nrm(ks[16], (N_ODD, HG_V, D), HG_V ** -0.5),
        "lb_logits": nrm(ks[17], (2, DEPTH_2 + 1, HG_K), 0.1),
    }

def second_block(x, c, ctx, c_ctx, ada_w, ada_b, pre_g, post_g, ev_w_in, ev_pool_w,
              ev_pool_scale, ev_conv_w, ev_conv_b, ev_w_out, od_w_in, od_onorm_g,
              od_w_out, lb_logits):
    lb_table = jnp.cumsum(jax.nn.softmax(lb_logits.astype(jnp.float32), axis=1), axis=1)
    s_lat = jax.nn.silu(c)
    s_ctx = jax.nn.silu(c_ctx)
    for layer in range(DEPTH_2):
        last = layer == DEPTH_2 - 1
        shift, scale, gate = jnp.split((s_lat @ ada_w[layer] + ada_b[layer])[:, None, :], 3, axis=-1)
        h = rms_norm(x, pre_g[layer]) * (1.0 + scale) + shift
        need_ctx = (layer % 2 == 1) or not last
        if need_ctx:
            shift_c, scale_c, gate_c = jnp.split(s_ctx @ ada_w[layer] + ada_b[layer], 3)
            hc = rms_norm(ctx, pre_g[layer]) * (1.0 + scale_c) + shift_c
        if layer % 2 == 0:
            e = layer // 2
            y = pool_conv_mixer(h, ev_w_in[e], ev_pool_w[e], ev_pool_scale[e], ev_conv_w[e],
                                ev_conv_b[e], ev_w_out[e], True)
            if not last:
                yc = pool_conv_mixer(hc, ev_w_in[e], ev_pool_w[e], ev_pool_scale[e], ev_conv_w[e],
                                     ev_conv_b[e], ev_w_out[e], False)
        else:
            o = layer // 2
            y, yc = hgrn2_mixer(h, hc, od_w_in[o], od_onorm_g[o], od_w_out[o],
                                lb_table[0, layer], lb_table[1, layer], not last)
        x = x + gate * rms_norm(y, post_g[layer])
        if not last:
            ctx = ctx + gate_c * rms_norm(yc, post_g[layer])
    return x


def setup_inputs(seed=0):
    out = dict(first_inputs(seed))
    for name, value in second_inputs(seed + 1).items():
        if name != "x":
            out[name + "_2"] = value
    return out


def reference(
    x, p, g_mix_pre, w_in, w_branch_a, w_branch_b, w_out, g_mix_post, g_ffn_pre, w_up, conv_w,
    conv_b, w_down, g_ffn_post, w_ple_in, w_ple_gate, c_2, ctx_2, c_ctx_2, ada_w_2, ada_b_2,
    pre_g_2, post_g_2, ev_w_in_2, ev_pool_w_2, ev_pool_scale_2, ev_conv_w_2, ev_conv_b_2,
    ev_w_out_2, od_w_in_2, od_onorm_g_2, od_w_out_2, lb_logits_2,
):
    x = first_block(
        x, p, g_mix_pre, w_in, w_branch_a, w_branch_b, w_out, g_mix_post, g_ffn_pre, w_up,
        conv_w, conv_b, w_down, g_ffn_post, w_ple_in, w_ple_gate,
    )
    return second_block(
        x, c_2, ctx_2, c_ctx_2, ada_w_2, ada_b_2, pre_g_2, post_g_2, ev_w_in_2, ev_pool_w_2,
        ev_pool_scale_2, ev_conv_w_2, ev_conv_b_2, ev_w_out_2, od_w_in_2, od_onorm_g_2,
        od_w_out_2, lb_logits_2,
    )


_drawn_inputs = setup_inputs


def setup_inputs(seed=0):
    import zlib

    import numpy as np

    out = dict(_drawn_inputs(seed))
    spreads = {}
    factors = {'conv_b': 6.645,
     'ctx_2': 4.322,
     'c_ctx_2': 5.385,
     'ada_b_2': 5.484,
     'post_g_2': 4.877,
     'ev_pool_scale_2': 5.483,
     'ev_conv_b_2': 33.071,
     'od_onorm_g_2': 7.424,
     'lb_logits_2': 4.428}
    for name, (base, spread) in spreads.items():
        noise = np.random.default_rng([zlib.crc32(name.encode()), seed]).standard_normal(out[name].shape)
        drawn = base * np.exp(spread * noise) if base else spread * noise
        out[name] = __import__('jax').numpy.asarray(drawn.astype(out[name].dtype))
    for name, factor in factors.items():
        out[name] = (out[name] * factor).astype(out[name].dtype)
    return out
```

```python
import numpy as np

import concourse.bass as bass
from concourse import mybir

F32 = mybir.dt.float32
F32R = mybir.dt.float32r
I32 = mybir.dt.int32
ALU = mybir.AluOpType
ACT = mybir.ActivationFunctionType
AX = mybir.AxisListType

D = 2048
T = 256
NT = D // 128
DFF = 5632
NF = DFF // 128
EPS = 1e-6
QS = 1.0 / float(np.sqrt(128.0))
RING, SPLIT, AHEAD = 5, 4, 3
ADA_GROUPS = [(l, g) for l in range(2) for g in range(12)]

VEC = {}


def _place():
    at = 0
    for name, n in (("g_mix_pre", 16), ("g_mix_post", 16), ("g_ffn_pre", 16), ("g_ffn_post", 16),
                    ("pre0", 16), ("pre1", 16), ("post0", 16), ("post1", 16), ("pscale", 8),
                    ("ecw", 24), ("ecb", 8), ("cw", 264), ("cb", 88), ("onorm", 16),
                    ("lb", 96), ("adab", 96), ("c", 32)):
        VEC[name] = at
        at += n
    return at


NVEC = _place()
CB = {"ident": 0, "tri": 128, "ms": 256, "rst": 128}
NCB = 640


def matmul(*a, **k):
    return lambda e: e.matmul(*a, **k)


def transpose(*a, **k):
    return lambda e: e.transpose(*a, **k)


def activation(*a, **k):
    return lambda e: e.activation(*a, **k)


def tensor_tensor(*a, **k):
    return lambda e: e.tensor_tensor(*a, **k)


def scalar_tensor_tensor(*a, **k):
    return lambda e: e.scalar_tensor_tensor(*a, **k)


def tensor_scalar(*a, **k):
    return lambda e: e.tensor_scalar(*a, **k)


def tensor_copy(*a, **k):
    return lambda e: e.tensor_copy(*a, **k)


def tensor_reduce(*a, **k):
    return lambda e: e.tensor_reduce(*a, **k)


def tensor_tensor_scan(*a, **k):
    return lambda e: e.tensor_tensor_scan(*a, **k)


def reciprocal(*a, **k):
    return lambda e: e.reciprocal(*a, **k)


def memset(*a, **k):
    return lambda e: e.memset(*a, **k)


def dma_start(*a, **k):
    return lambda e: e.dma_start(*a, **k)


class Lane:

    def __init__(self, sem):
        self.sem, self.n, self.items = sem, 0, []

    def wait(self, *toks):
        self.items += [("wait", t) for t in toks if t is not None]

    def run(self, fn):
        self.items.append(("run", fn))

    def sig(self, fn):
        self.n += 1
        self.items.append(("sig", fn, self.sem, 1))
        return (self.sem, self.n)

    def sig_on(self, fn, sem, by):
        self.items.append(("sig", fn, sem, by))

    def mark(self):
        sub = []
        self.items.append(("sub", sub))
        return sub

    def play(self, eng, items=None, seen=None):
        items = self.items if items is None else items
        seen = {} if seen is None else seen
        for it in items:
            if it[0] == "wait":
                sem, n = it[1]
                if seen.get(id(sem), 0) < n:
                    eng.wait_ge(sem, n)
                    seen[id(sem)] = n
            elif it[0] == "run":
                it[1](eng)
            elif it[0] == "sig":
                it[1](eng).then_inc(it[2], it[3])
            else:
                self.play(eng, it[1], seen)


class Operand:

    def __init__(self, hi, lo, n, make=None, toks=None, ahead=0):
        self.hi, self.lo, self.n, self.make, self.ahead = hi, lo, n, make, ahead
        self.toks = list(toks or [])

    def need(self, k):
        if self.make is not None:
            while len(self.toks) <= min(k + self.ahead, self.n - 1):
                self.toks.append(self.make(len(self.toks)))
        return self.toks[k] if k < len(self.toks) else None


class Program:
    def __init__(self, nc, A):
        self.nc, self.A = nc, A
        s = nc.alloc_semaphore
        self.act, self.dve, self.pe = Lane(s("act")), Lane(s("dve")), Lane(s("pe"))
        self.pool, self.sp = Lane(s("pool")), Lane(s("sp"))
        self.s_raw = [s(f"raw{i}") for i in range(RING)]
        self.s_hi, self.s_lo, self.s_mm = s("hi"), s("lo"), s("mm")
        self.s_ld = {}
        self.base = (nc.sbuf_base + 31) // 32 * 32
        self.names = set()
        self.chunks = []
        self.marks = []
        self.nsplit = 0
        self.split_pe = []
        self.set_at = 0
        self.set_free = [[], []]
        self.bank_free = {b: [] for b in range(4, 8)}
        self.gens = []
        self.serial = False
        self.ada_at = 0
        self.pending = None
        self.ada_rate = 0.0
        self.ada_due = 0.0
        self.PS = [nc.alloc_psum_tensor(f"ps{i}", [128, 512], F32) for i in range(8)]
        at = 0
        self.raw = [self.sb(f"raw_{i}", [128, 1024], F32, at + 4 * i) for i in range(RING)]
        at += 4 * RING
        self.whi = [self.sb(f"whi{i}", [128, 1024], F32R, at + 4 * i) for i in range(SPLIT)]
        at += 4 * SPLIT
        self.wlo = [self.sb(f"wlo{i}", [128, 1024], F32R, at + 4 * i) for i in range(SPLIT)]
        at += 4 * SPLIT
        self.vec = self.sb("vec", [128, NVEC], F32, at)
        at += 3
        self.cst = self.sb("cst", [128, NCB], F32, at)
        at += 2.5
        self.R = self.sb("R", [128, 512], F32, at)
        at += 2
        self.ones = self.sb("ones", [128, 128], F32, at)
        self.hgm = self.sb("hgm", [128, 256], I32, at + 0.5)
        at += 1.5
        self.M = self.sb("M", [128, 2 * 2 * 48], F32, at)
        self.G = self.sb("G", [128, 128], F32, at + 0.75)
        self.S = self.sb("S", [128, 32], F32, at + 1.25)
        self.LB = self.sb("LB", [128, 64], F32, at + 1.375)
        self.DEC = self.sb("DEC", [128, 16], F32, at + 1.625)
        self.SM = self.sb("SM", [128, 64], F32, at + 1.75)
        at += 2
        self.P0 = at
        self.H = self.sb("H", [128, NT, T], F32, at)
        self.F = at + 16

    def sb(self, name, shape, dt, kb):
        off = self.base + int(round(kb * 1024))
        return self.nc.alloc_sbuf_tensor_at(name, shape, dt, offset=off)

    def v(self, name, k=0, n=1):
        a = VEC[name] + k
        return self.vec[:, a:a + n]

    def load(self, dst, src, name, after=()):
        sem = self.s_ld.get(name)
        if sem is None:
            sem = [self.nc.alloc_semaphore(f"ld_{name}"), 0]
            self.s_ld[name] = sem
        self.pool.wait(*after)
        sem[1] += 16
        self.pool.sig_on(dma_start(dst, src), sem[0], 16)
        return (sem[0], sem[1])

    def chunk(self, src, kt, cols, split):
        c = len(self.chunks)
        slot, use = c % RING, c // RING
        n = kt * cols
        raw = self.raw[slot][:, 0:n]
        landed = (self.s_raw[slot], 16 * (use + 1))
        self.marks.append((self.act.mark(), self.dve.mark()))
        ch = {"src": src, "dst": raw.rearrange("p (k c) -> p k c", k=kt)}
        if split:
            i = self.nsplit
            self.nsplit += 1
            hi, lo = self.whi[i % SPLIT][:, 0:n], self.wlo[i % SPLIT][:, 0:n]
            ma, md = self.marks[max(c - AHEAD, 0)]
            ma.append(("wait", landed))
            if i >= SPLIT:
                ma.append(("wait", self.split_pe[i - SPLIT]))
            ma.append(("sig", activation(hi, raw, ACT.Copy), self.s_hi, 1))
            md.append(("wait", landed))
            md.append(("wait", (self.s_hi, i + 1)))
            md.append(("sig", tensor_tensor(lo, raw, hi.bitcast(F32), ALU.subtract), self.s_lo, 1))
            ch["ready"] = (self.s_lo, i + 1)
            ch["hi"] = hi.rearrange("p (k c) -> p k c", k=kt)
            ch["lo"] = lo.rearrange("p (k c) -> p k c", k=kt)
            ch["free"] = (self.s_lo, i + 1)
            self.split_pe.append((self.s_mm, c + 1))
        else:
            ch["ready"] = landed
            ch["hi"] = ch["dst"]
            ch["free"] = (self.s_mm, c + 1)
        self.chunks.append(ch)
        return ch

    def play_stream(self):
        for c, ch in enumerate(self.chunks):
            if c >= RING:
                self.sp.wait(self.chunks[c - RING]["free"])
            self.sp.sig_on(dma_start(ch["dst"], ch["src"]), self.s_raw[c % RING], 16)

    def pump(self):
        for g in self.gens[0:1] if self.serial else list(self.gens):
            if next(g, "end") == "end":
                self.gens.remove(g)

    def finish(self, *gens):
        for g in gens or list(self.gens):
            while g in self.gens:
                h = self.gens[0] if self.serial else g
                if next(h, "end") == "end":
                    self.gens.remove(h)

    def tiles(self, s, width):
        per = 512 // width
        return lambda i: self.PS[2 * s + i // per][:, (i % per) * width:(i % per + 1) * width]

    def group(self, W, c0, cols, X, N, tm=False, raw=False, quiet=False):
        K = X.n
        kt = min(K, 1024 // cols)
        s = self.set_at % 2
        self.set_at += 1
        width = cols if tm else N
        out, per = self.tiles(s, width), 512 // width
        count = N // 128 if tm else cols // 128
        for j in range(K // kt):
            src = W[j * kt * 128:(j + 1) * kt * 128, c0:c0 + cols].rearrange("(k p) c -> p k c", p=128)
            c = len(self.chunks)
            ch = self.chunk(src, kt, cols, not raw)
            self.pump()
            for k in range(j * kt, (j + 1) * kt):
                X.need(k)
            self.pe.wait(ch["ready"])
            if j == 0:
                self.pe.wait(*self.set_free[s])
            for k in range(kt):
                kk = j * kt + k
                if self.serial and N == 512 and 2 * k == kt:
                    self.pump()
                self.pe.wait(X.need(kk))
                for i in range(count):
                    first = kk == 0 and i % per == 0
                    if tm:
                        cut = slice(i * 128, (i + 1) * 128)
                        xs = [X.hi(kk)[:, cut]] + ([] if raw else [X.lo(kk)[:, cut]])
                        ws = [ch["hi"][:, k, :]] + ([] if raw else [ch["lo"][:, k, :]])
                        terms = [(xs[0], ws[0])] + ([] if raw else [(xs[1], ws[0]), (xs[0], ws[1])])
                    else:
                        cut = slice(i * 128, (i + 1) * 128)
                        xs = [X.hi(kk)] + ([] if raw else [X.lo(kk)])
                        ws = [ch["hi"][:, k, cut]] + ([] if raw else [ch["lo"][:, k, cut]])
                        terms = [(ws[0], xs[0])] + ([] if raw else [(ws[1], xs[0]), (ws[0], xs[1])])
                    for t, (a, b) in enumerate(terms):
                        last = kk == K - 1 and t == len(terms) - 1
                        o = out(i)
                        fn = matmul(o, a, b, start=first and t == 0, stop=last, skip_group_check=True)
                        if k == kt - 1 and i == count - 1 and t == len(terms) - 1:
                            self.pe.sig_on(fn, self.s_mm, 1)
                        else:
                            self.pe.run(fn)
            if not quiet:
                self.ada_due += self.ada_rate
                while self.ada_due >= 1:
                    self.ada_due -= 1
                    self.ada(1)
        return s, (self.s_mm, c + 1)

    def ada(self, n):
        for _ in range(n):
            if self.ada_at >= 8 * len(ADA_GROUPS):
                return
            g, j = divmod(self.ada_at, 8)
            self.ada_at += 1
            l, m = ADA_GROUPS[g]
            bank = 6 + g % 2
            W = self.A["ada_w"][l]
            src = W[j * 256:(j + 1) * 256, m * 512:(m + 1) * 512].rearrange("(k p) c -> p k c", p=128)
            c = len(self.chunks)
            ch = self.chunk(src, 2, 512, False)
            self.pe.wait(ch["ready"])
            if j == 0:
                self.pe.wait(*self.bank_free[bank])
                self.pe.wait(self.tk["S"])
            for k in range(2):
                n = 2 * j + k
                r = 32 * (n % 4)
                fn = matmul(self.PS[bank][r:r + 2, :], self.S[:, 2 * n:2 * n + 2], ch["hi"][:, k, :],
                            start=n < 4, stop=n >= 12, skip_group_check=True)
                if k == 1:
                    self.pe.sig_on(fn, self.s_mm, 1)
                else:
                    self.pe.run(fn)
            if j == 7:
                self.act.wait((self.s_mm, c + 1), self.tk.get("Rfree"))
                t = self.act.sig(activation(self.R[:, :], self.PS[bank][:, :], ACT.Copy))
                self.bank_free[bank] = [t]
                self.pending = (g, t)
            elif j == 1 and self.pending:
                self.ada_end()

    def ada_end(self):
        g, t = self.pending
        self.pending = None
        l, m = ADA_GROUPS[g]
        bank = 6 + g % 2
        self.pe.wait(t)
        for i in range(4):
            u = self.pe.sig(transpose(self.PS[bank][:, 128 * i:128 * i + 128], self.R[:, 128 * i:128 * i + 128],
                                      self.cst[:, 0:128]))
        self.tk["Rfree"] = u
        self.dve.wait(u)
        for w in range(2):
            a = (l * 2 + w) * 48 + 4 * m
            v = self.PS[bank][:, :].rearrange("p (i j q) -> p i q j", i=4, j=4)[:, :, w, :]
            tok = self.dve.sig(tensor_reduce(self.M[:, a:a + 4], v, AX.X, ALU.add))
        self.bank_free[bank] = [tok]
        self.dve.wait(tok)
        for w in range(2):
            a = (l * 2 + w) * 48 + 4 * m
            tok = self.dve.sig(tensor_tensor(self.M[:, a:a + 4], self.M[:, a:a + 4],
                                             self.v("adab", l * 48 + 4 * m, 4), ALU.add))
        self.tk["M"] = tok

    def mods(self, l):
        if self.pending:
            self.ada_end()
        d, g0 = self.dve, 64 * l
        d.wait(self.tk["M"])
        for w in range(2):
            a = (l * 2 + w) * 48
            t = d.sig(scalar_tensor_tensor(
                self.G[:, g0 + 16 * w:g0 + 16 * w + 16], self.M[:, a + 16:a + 32], 1.0,
                self.v(f"pre{l}", 0, 16), ALU.add, ALU.mult))
            t = d.sig(tensor_tensor(
                self.G[:, g0 + 32 + 16 * w:g0 + 48 + 16 * w], self.M[:, a + 32:a + 48],
                self.v(f"post{l}", 0, 16), ALU.mult))
        self.tk["G"] = t

    def shift(self, l, w, k):
        a = (l * 2 + w) * 48 + k
        return self.M[:, a:a + 1]

    def coef(self, l, what, w, k):
        a = 64 * l + 32 * what + 16 * w + k
        return self.G[:, a:a + 1]

    def norm_buffers(self, tag, kb, width):
        b = {"sq": [self.sb(f"sq{tag}{i}", [128, 512], F32, kb + 2 * i) for i in range(2)],
             "acc": self.sb(f"acc{tag}", [128, 512], F32, kb + 4),
             "rs": self.sb(f"rs{tag}", [128, 512], F32, kb + 6),
             "t": [self.sb(f"t{tag}{i}", [128, width], F32, kb + 8 + i * width / 256) for i in range(3)],
             "sqr": [None, None], "n": 0, "width": width, "acct": None, "tfree": {}}
        return b

    def sq_add(self, b, src, first, after, eng=None):
        i = b["n"] % 2
        b["n"] += 1
        self.act.wait(*after)
        self.act.wait(b["sqr"][i])
        t = self.act.sig(activation(b["sq"][i][:, :], src, ACT.Square))
        self.dve.wait(t)
        self.dve.wait(b["acct"])
        if first:
            u = self.dve.sig(tensor_copy(b["acc"][:, :], b["sq"][i][:, :]))
        else:
            u = self.dve.sig(tensor_tensor(b["acc"][:, :], b["acc"][:, :], b["sq"][i][:, :], ALU.add))
        b["sqr"][i] = b["acct"] = u
        return t

    def rstd(self, b, N, scale, bank=5):
        self.pe.wait(b["acct"], self.tk["ones"], *self.bank_free[bank])
        ps = self.PS[bank][:, 0:N]
        if N == 256:
            self.pe.run(matmul(ps, self.ones[:, :], b["acc"][:, 0:256], start=True, stop=False))
            p = self.pe.sig(matmul(ps, self.ones[:, :], b["acc"][:, 256:512], start=False, stop=True))
        else:
            p = self.pe.sig(matmul(ps, self.ones[:, :], b["acc"][:, :], start=True, stop=True))
        rs = b["rs"][:, 0:N]
        self.dve.wait(p, *b["tfree"].values())
        t = self.dve.sig(tensor_scalar(rs, ps, scale, EPS, ALU.mult, ALU.add))
        self.bank_free[bank] = [t]
        self.act.wait(t)
        t = self.act.sig(activation(rs, rs, ACT.Sqrt))
        self.dve.wait(t)
        t = self.dve.sig(reciprocal(rs, rs))
        self.dve.wait(t)
        b["acct"] = p
        return t

    def scaled(self, b, src, coef, shift, hi, lo, c0, N):
        pend = []

        def flush():
            for t, k, h in pend:
                self.dve.wait(h)
                if shift is None:
                    u = self.dve.sig(tensor_tensor(
                        lo(k), t, hi(k).bitcast(F32), ALU.subtract))
                else:
                    u = self.dve.sig(scalar_tensor_tensor(
                        lo(k), t, shift(k), hi(k).bitcast(F32), ALU.add, ALU.subtract))
                res[k] = u
                b["tfree"][k % 3, c0] = u
            pend.clear()

        res = {}

        def start(k):
            t = b["t"][k % 3][:, c0:c0 + N]
            self.dve.wait(b["tfree"].get((k % 3, c0)))
            d = self.dve.sig(scalar_tensor_tensor(
                t, src(k), coef(k), b["rs"][:, c0:c0 + N], ALU.mult, ALU.mult))
            self.act.wait(d)
            if shift is None:
                h = self.act.sig(activation(hi(k), t, ACT.Copy))
            else:
                h = self.act.sig(activation(hi(k), t, ACT.Identity, bias=shift(k)))
            return (t, k, h)

        begun = []

        def make(k):
            while len(begun) <= min(k + 1, NT - 1):
                begun.append(start(len(begun)))
            pend.append(begun[k])
            flush()
            return res[k]
        return make


def halves(p, name, n, width, kb):
    hi = p.sb(name + "h", [128, n, width], F32R, kb)
    lo = p.sb(name + "l", [128, n, width], F32R, kb + n * width / 256)
    return hi, lo


def tile_of(t, a=None, b=None):
    if a is None:
        return lambda k: t[:, k, :]
    return lambda k: t[:, k, a:b]


def late_split(p, src, hi, lo, n, ready):
    def make(k):
        p.act.wait(*ready)
        h = p.act.sig(activation(hi(k), src(k), ACT.Copy))
        p.dve.wait(h, *ready)
        return p.dve.sig(tensor_tensor(lo(k), src(k), hi(k).bitcast(F32), ALU.subtract))
    return Operand(hi, lo, n, make, ahead=2)


def attention_a(p, q, k, v, sb):
    act, dve, pe, PS = p.act, p.dve, p.pe, p.PS
    Sx, PT, st = sb["S"], sb["PT"], sb["st"]
    for h in range(4):
        for qb in range(2):
            nk = 128 * (qb + 1)
            pe.wait(*p.tk["qkv"], *p.bank_free[4], *p.bank_free[5])
            for g in range(3):
                o = PS[4 + g // 2][:, (g % 2) * 256:(g % 2) * 256 + nk]
                f = (matmul(o, q[:, 4 * g + h, qb * 128:qb * 128 + 128],
                                                  k[:, 4 * g + h, 0:nk], start=True, stop=True,
                                                  skip_group_check=True))
                t = pe.sig(f)
            yield
            dve.wait(t, p.tk.get("Sfree"), p.tk["cst"])
            for g in range(3):
                o = PS[4 + g // 2][:, (g % 2) * 256:(g % 2) * 256 + nk]
                slope = float(np.float32(2.0) ** np.float32(-8.0 * (4 * g + h + 1) / 12))
                t = dve.sig(scalar_tensor_tensor(
                    Sx[:, g, 0:nk], sb["bias"][:, g, qb, 0:nk], slope, o, ALU.mult, ALU.add))
            p.bank_free[4] = p.bank_free[5] = [t]
            dve.wait(t)
            t = dve.sig(tensor_reduce(st[:, 0:1], Sx[:, :, 0:nk], AX.XY, ALU.max))
            dve.wait(t)
            t = dve.sig(tensor_scalar(st[:, 1:2], st[:, 0:1], -1.0, None, ALU.mult))
            act.wait(t)
            t = act.sig(activation(Sx[:, :, 0:nk], Sx[:, :, 0:nk], ACT.Exp, bias=st[:, 1:2],
                                               accum_out=st[:, 2:3]))
            yield
            dve.wait(t)
            t = dve.sig(reciprocal(st[:, 3:4], st[:, 2:3]))
            dve.wait(t)
            t = dve.sig(tensor_scalar(Sx[:, :, 0:nk], Sx[:, :, 0:nk], st[:, 3:4], None, ALU.mult))
            yield
            pe.wait(t, *p.bank_free[4], *p.bank_free[5])
            blocks = [(g, kb) for g in range(3) for kb in range(qb + 1)]
            for i, (g, kb) in enumerate(blocks):
                o = PS[4 + i // 4][:, (i % 4) * 128:(i % 4) * 128 + 128]
                t = pe.sig(transpose(
                    o, Sx[:, g, kb * 128:kb * 128 + 128], p.cst[:, 0:128]))
            p.tk["Sfree"] = t
            act.wait(t, p.tk.get("PTfree"))
            n0 = min(len(blocks), 4) * 128
            t = act.sig(activation(PT[:, 0:n0], PS[4][:, 0:n0], ACT.Copy))
            p.bank_free[4] = [t]
            if len(blocks) > 4:
                n1 = len(blocks) * 128 - 512
                t = act.sig(activation(PT[:, 512:512 + n1], PS[5][:, 0:n1], ACT.Copy))
                p.bank_free[5] = [t]
            yield
            pe.wait(t, *p.bank_free[6])
            for i, (g, kb) in enumerate(blocks):
                c0 = (4 * g + h) * 128
                t = pe.sig(matmul(
                    PS[6][:, 0:128], v[:, kb, c0:c0 + 128], PT[:, i * 128:i * 128 + 128],
                    start=(i == 0), stop=(i == len(blocks) - 1), skip_group_check=True))
            p.tk["PTfree"] = t
            act.wait(t)
            t = act.sig(activation(sb["ya"][:, h, qb * 128:qb * 128 + 128], PS[6][:, 0:128], ACT.Copy))
            p.bank_free[6] = [t]
            p.tk["ya"] = t
            yield


def attention_b(p, q, k, v, sb):
    act, dve, pe, PS = p.act, p.dve, p.pe, p.PS
    Z, E, R = sb["z"], sb["e"], sb["r"]
    ms = p.cst[:, CB["ms"]:CB["ms"] + 384]
    tri = p.cst[:, CB["tri"]:CB["tri"] + 128]
    B = PS[7]
    for h in range(4):
        pe.wait(*p.tk["qkv"], *p.bank_free[7])
        pe.run(matmul(B[:, 0:256], k[:, h, 0:128], q[:, h, :], start=True, stop=True,
                                  skip_group_check=True))
        t = pe.sig(matmul(B[:, 256:384], k[:, h, 128:256], q[:, h, 128:256], start=True, stop=True,
                                      skip_group_check=True))
        yield
        dve.wait(t, p.tk["cst"])
        z = dve.sig(tensor_copy(Z[:, :], B[:, 0:384]))
        act.wait(z)
        t = act.sig(activation(E[:, :], Z[:, :], ACT.Abs))
        act.wait(t)
        t = act.sig(activation(E[:, :], E[:, :], ACT.Exp, scale=-1.0))
        act.wait(t)
        l = act.sig(activation(E[:, :], E[:, :], ACT.Ln, bias=1.0))
        yield
        dve.wait(l, z)
        t = dve.sig(scalar_tensor_tensor(R[:, :], Z[:, :], 0.0, E[:, :], ALU.max, ALU.add))
        dve.wait(t)
        t2 = dve.sig(tensor_tensor(Z[:, :], Z[:, :], R[:, :], ALU.subtract))
        t = dve.sig(tensor_tensor(R[:, :], R[:, :], ms, ALU.mult))
        yield
        pe.wait(t)
        pe.run(matmul(B[:, 0:256], tri, R[:, 0:256], start=True, stop=True, skip_group_check=True))
        pe.run(matmul(B[:, 128:256], p.ones[:, :], R[:, 256:384], start=False, stop=True,
                                  skip_group_check=True))
        t = pe.sig(matmul(B[:, 256:384], tri, R[:, 256:384], start=False, stop=True,
                                      skip_group_check=True))
        yield
        dve.wait(t, t2)
        t = dve.sig(tensor_tensor(Z[:, :], Z[:, :], B[:, 0:384], ALU.subtract))
        act.wait(t)
        t = act.sig(activation(Z[:, :], Z[:, :], ACT.Exp))
        dve.wait(t)
        t = dve.sig(tensor_tensor(Z[:, :], Z[:, :], ms, ALU.mult))
        yield
        pe.wait(t)
        pe.run(matmul(B[:, 0:256], v[:, 0, h * 128:h * 128 + 128], Z[:, 0:256], start=True, stop=True,
                                  skip_group_check=True))
        t = pe.sig(matmul(B[:, 128:256], v[:, 1, h * 128:h * 128 + 128], Z[:, 256:384],
                                      start=False, stop=True, skip_group_check=True))
        yield
        act.wait(t)
        dve.wait(t)
        t = act.sig(activation(sb["yb"][:, h, :], B[:, 0:256], ACT.Copy))
        p.bank_free[7] = [t]
        p.tk["yb"] = t
        yield


def first_block(p):
    act, dve, pe, PS, A, F = p.act, p.dve, p.pe, p.PS, p.A, p.F
    H = p.H
    nb = p.norm_buffers("a", F + 80, 256)
    Uh, Ul = halves(p, "U", NT, T, F)
    for i in range(8):
        src = H[:, 2 * i:2 * i + 2, :]
        p.sq_add(nb, src, i == 0, [p.tk["x"]])
    dve.wait(p.tk["x"], p.tk["vec"])
    p.rstd(nb, 256, 1.0 / D)
    U = Operand(tile_of(Uh), tile_of(Ul), NT,
                p.scaled(nb, tile_of(H), lambda k: p.v("g_mix_pre", k), None, tile_of(Uh), tile_of(Ul), 0, T),
                ahead=3)
    b = F + 32
    qa = p.sb("qa", [128, 12, T], F32, b)
    ka = p.sb("ka", [128, 12, T], F32, b + 12)
    va = p.sb("va", [128, 2, 1536], F32, b + 24)
    qb_ = p.sb("qb", [128, 4, T], F32, b + 36)
    kb_ = p.sb("kb", [128, 4, T], F32, b + 40)
    vb = p.sb("vb", [128, 2, 512], F32, b + 44)
    W = A["w_in"]
    toks = []

    def plain(dst, scale):
        def evac(s, t):
            act.wait(t)
            for i in range(2):
                u = act.sig(activation(dst(i), PS[2 * s + i][:, :], ACT.Copy, scale=scale))
            p.set_free[s] = [u]
            toks.append(u)
        return evac

    def fm(t, m):
        return lambda i: t[:, m + 2 * i:m + 2 * i + 2, :]

    for g in range(20 - 8):
        tm = g in (6, 7, 8, 11)
        s, t = p.group(W, g * 512, 512, U, T, tm=tm)
        if g < 3:
            plain(fm(qa, 4 * g), QS)(s, t)
        elif g < 6:
            plain(fm(ka, 4 * (g - 3)), 1.0)(s, t)
        elif g < 9:
            plain(lambda i, g=g: va[:, i, (g - 6) * 512:(g - 5) * 512], 1.0)(s, t)
        elif g == 9:
            plain(fm(qb_, 0), QS)(s, t)
        elif g == 10:
            plain(fm(kb_, 0), 1.0)(s, t)
        else:
            plain(lambda i: vb[:, i, :], 1.0)(s, t)
    p.tk["qkv"] = toks[-1:]
    b = F + 80
    gt = p.sb("gt", [128, 32, T], F32, b)
    bias = p.sb("bias", [128, 3, 2, 256], F32, b + 32)
    sbx = {"bias": bias, "ya": qa, "yb": qb_,
           "S": p.sb("Sx", [128, 3, 256], F32, b + 38), "PT": p.sb("PT", [128, 768], F32, b + 41),
           "z": p.sb("z", [128, 384], F32, b + 44), "e": p.sb("e", [128, 384], F32, b + 45.5),
           "r": p.sb("r", [128, 384], F32, b + 47), "st": p.SM}
    p.tk["cst"] = p.load(bias[:, :, :, :], A["bias"].rearrange("p (a b c) -> p a b c", a=3, b=2), "bias",
                         [toks[-1]])
    p.gens = [attention_a(p, qa, ka, va, sbx), attention_b(p, qb_, kb_, vb, sbx)]
    for g in range(8):
        s, t = p.group(W, 6144 + g * 512, 512, U, T)
        act.wait(t)
        for i in range(2):
            u = act.sig(activation(gt[:, 4 * g + 2 * i:4 * g + 2 * i + 2, :],
                                                    PS[2 * s + i][:, :], ACT.Copy))
        p.set_free[s] = [u]
    gate_done = t
    p.finish()
    for b in (6, 7):
        dve.wait(*p.bank_free[b])
        p.bank_free[b] = [dve.sig(memset(PS[b][:, :], 0.0))]
    p.tk["rst"] = p.load(p.cst[:, 128:640], A["cst"][:, 640:1152], "rst", [p.tk["ya"], p.tk["yb"], p.bank_free[7][0]])
    YAh, YAl = halves(p, "YA", 4, T, F)
    YBh, YBl = halves(p, "YB", 4, T, F + 8)
    act.wait(gate_done)
    dve.wait(gate_done)
    YA = late_split(p, tile_of(qa), tile_of(YAh), tile_of(YAl), 4, [p.tk["ya"]])
    YB = late_split(p, tile_of(qb_), tile_of(YBh), tile_of(YBl), 4, [p.tk["yb"]])
    YA.ahead = YB.ahead = 3
    YA.need(3)
    YB.need(3)
    MIX = halves(p, "MIX", NT, T, F + 32)
    t1 = p.sb("mt1", [128, 1024], F32, F + 120)
    t2 = p.sb("mt2", [128, 1024], F32, F + 124)
    mtoks = []
    act.wait(u)
    for i in range(8):
        u = act.sig(activation(gt[:, 4 * i:4 * i + 4, :], gt[:, 4 * i:4 * i + 4, :], ACT.Sigmoid))
    sig = u
    mixfree = None
    for g in range(4):
        sa, ta = p.group(A["w_ba"], g * 512, 512, YA, T)
        sb_, tb = p.group(A["w_bb"], g * 512, 512, YB, T)
        dve.wait(ta, sig, mixfree)
        for i in range(2):
            u = dve.sig(tensor_tensor(t1[:, 512 * i:512 * i + 512], PS[2 * sa + i][:, :],
                                                       gt[:, 4 * g + 2 * i:4 * g + 2 * i + 2, :], ALU.mult))
        p.set_free[sa] = [u]
        dve.wait(tb)
        for i in range(2):
            u = dve.sig(tensor_tensor(t2[:, 512 * i:512 * i + 512], PS[2 * sb_ + i][:, :],
                                                       gt[:, 16 + 4 * g + 2 * i:18 + 4 * g + 2 * i, :], ALU.mult))
        p.set_free[sb_] = [u]
        dve.wait(u)
        u = dve.sig(tensor_tensor(t1[:, :], t1[:, :], t2[:, :], ALU.add))
        act.wait(u)
        h = act.sig(activation(MIX[0][:, 4 * g:4 * g + 4, :], t1[:, :], ACT.Copy))
        dve.wait(h, u)
        u = dve.sig(tensor_tensor(MIX[1][:, 4 * g:4 * g + 4, :], t1[:, :],
                                                   MIX[0][:, 4 * g:4 * g + 4, :].bitcast(F32), ALU.subtract))
        mixfree = u
        mtoks += [u] * 4
    p.ada_rate = ADA1
    X = Operand(tile_of(MIX[0]), tile_of(MIX[1]), NT, toks=mtoks)
    Y = p.sb("Yw", [128, NT, T], F32, F + 64)
    nb = p.norm_buffers("b", F + 104, 256)
    out_groups(p, A["w_out"], X, Y, nb, T, 512, after=[mtoks[-1]])
    run_beside(p, residual(p, Y, nb, T, [(H, lambda k: p.v("g_mix_post", k), 0)], True), 14)
    Uh, Ul = halves(p, "V", NT, T, F)
    U = Operand(tile_of(Uh), tile_of(Ul), NT,
                p.scaled(nb, tile_of(H), lambda k: p.v("g_ffn_pre", k), None, tile_of(Uh), tile_of(Ul), 0, T),
                ahead=3)
    AC = halves(p, "AC", NF, T, F + 32)
    cg = p.sb("cg", [128, 4, T], F32, F + 120)
    cv = p.sb("cv", [128, 4, T], F32, F + 124)
    atoks = []
    prod = None
    for g in range(11):
        for half, buf in ((0, cg), (1, cv)):
            s, t = p.group(A["w_up"], half * DFF + g * 512, 512, U, T)
            act.wait(t, prod)
            for i in range(4):
                m = half * NF + 4 * g + i
                o = PS[2 * s + i // 2][:, (i % 2) * 256:(i % 2) * 256 + 256]
                u = act.sig(activation(
                    buf[:, i, :], o, ACT.Identity, scale=p.v("cw", 176 + m), bias=p.v("cb", m)))
            dve.wait(u)
            for n in (1, 2):
                for i in range(4):
                    m = half * NF + 4 * g + i
                    o = PS[2 * s + i // 2][:, (i % 2) * 256:(i % 2) * 256 + 256 - n]
                    w = dve.sig(scalar_tensor_tensor(
                        buf[:, i, n:], o, p.v("cw", (2 - n) * 88 + m), buf[:, i, n:], ALU.mult, ALU.add))
                if n == 1:
                    dve.wait(w)
            p.set_free[s] = [w]
            if half == 0:
                act.wait(w)
                gel = act.sig(activation(cg[:, :, :], cg[:, :, :], ACT.Gelu_apprx_tanh))
        dve.wait(gel, w)
        u = dve.sig(tensor_tensor(cv[:, :, :], cg[:, :, :], cv[:, :, :], ALU.mult))
        act.wait(u)
        h = act.sig(activation(AC[0][:, 4 * g:4 * g + 4, :], cv[:, :, :], ACT.Copy))
        dve.wait(h, u)
        prod = dve.sig(tensor_tensor(AC[1][:, 4 * g:4 * g + 4, :], cv[:, :, :],
                                                      AC[0][:, 4 * g:4 * g + 4, :].bitcast(F32), ALU.subtract))
        atoks += [prod] * 4
    X = Operand(tile_of(AC[0]), tile_of(AC[1]), NF, toks=atoks)
    Y = p.sb("Yd", [128, NT, T], F32, F)
    nb = p.norm_buffers("c", F + 16, 256)
    down = out_groups(p, A["w_down"], X, Y, nb, T, 512, after=[prod])
    PF = p.sb("PF", [128, 2, T], F32, F + 120)
    E = p.sb("E", [128, NT, T], F32, F + 96)
    ptok = p.load(PF[:, :, :], A["pT"].rearrange("(k p) t -> p k t", p=128), "pf", [prod])
    XP = Operand(tile_of(PF), None, 2, toks=[ptok] * 2)
    p.gens = [residual(p, Y, nb, T, [(H, lambda k: p.v("g_ffn_post", k), 0)], False)]
    for g in range(4):
        s, t = p.group(A["w_ple_in"], g * 512, 512, XP, T, raw=True, quiet=True)
        act.wait(t, down)
        for i in range(2):
            u = act.sig(activation(E[:, 4 * g + 2 * i:4 * g + 2 * i + 2, :],
                                                         PS[2 * s + i][:, :], ACT.Copy))
        p.set_free[s] = [u]
        p.ada(2)
    etok = u
    run_beside(p, None, 6)
    p.finish()
    HC = halves(p, "HC", NT, 2 * T, F + 32)
    hh, hl = tile_of(HC[0], 0, T), tile_of(HC[1], 0, T)
    X = late_split(p, tile_of(H), hh, hl, NT, [p.tk["H"], down])
    CX = p.sb("CX", [128, NT, T], F32, F + 112)
    p.tk["cx"] = p.load(CX[:, :, :], A["ctxT"].rearrange("(k p) t -> p k t", p=128), "cx",
                        [down, etok, p.tk["pe_p"]] if "pe_p" in p.tk else [down, etok, t])
    tmp = p.sb("ptmp", [128, 1024], F32, F + 16 + 16)
    tmp = p.sb("ptmp2", [128, 1024], F32, F)
    last = None
    for g in range(4):
        s, t = p.group(A["w_ple_gate"], g * 512, 512, X, T)
        act.wait(t, last)
        for i in range(2):
            u = act.sig(activation(tmp[:, 512 * i:512 * i + 512], PS[2 * s + i][:, :], ACT.Sigmoid))
        p.set_free[s] = [u]
        dve.wait(u, etok)
        u = dve.sig(tensor_tensor(tmp[:, :], tmp[:, :], E[:, 4 * g:4 * g + 4, :], ALU.mult))
        dve.wait(u)
        last = dve.sig(tensor_tensor(H[:, 4 * g:4 * g + 4, :], H[:, 4 * g:4 * g + 4, :],
                                                      tmp[:, :], ALU.add))
        if g == 0:
            ctx_norm = None
    p.tk["H"] = last
    p.tk["hpe"] = t
    return HC, CX


def out_groups(p, W, X, Y, nb, N, cols, after=()):
    per = cols // 128
    for g in range(D // cols):
        s, t = p.group(W, g * cols, cols, X, N)
        p.act.wait(t, *after)
        for i in range(2):
            k = g * per + i * (512 // N)
            ps = p.PS[2 * s + i][:, :]
            p.act.run(activation(Y[:, k:k + 512 // N, :], ps, ACT.Copy))
            u = p.sq_add(nb, ps, g == 0 and i == 0, [])
        p.set_free[s] = [u]
    p.tk["Y"] = u
    return t


def residual(p, Y, nb, N, parts, again):
    yield
    p.rstd(nb, N, 1.0 / D)
    yield
    p.dve.wait(p.tk["Y"])
    n = 0
    for k in range(0, NT, 4):
        for Hh, coef, c0 in parts:
            for i in range(k, k + 4):
                u = p.dve.sig(scalar_tensor_tensor(
                    Y[:, i, c0:c0 + T], Y[:, i, c0:c0 + T], coef(i), nb["rs"][:, c0:c0 + T], ALU.mult, ALU.mult))
            p.dve.wait(u)
            h = p.dve.sig(tensor_tensor(
                Hh[:, k:k + 4, :], Hh[:, k:k + 4, :], Y[:, k:k + 4, c0:c0 + T], ALU.add))
            if again and N == 256:
                for i in (k, k + 2):
                    p.sq_add(nb, Hh[:, i:i + 2, :], i == 0, [h])
            yield
        if again and N == 512:
            for i in range(k, k + 4):
                j = nb["n"] % 2
                nb["n"] += 1
                p.act.wait(h, nb["sqr"][j])
                for m, (Hh, _, c0) in enumerate(parts):
                    t = p.act.sig(activation(
                        nb["sq"][j][:, c0:c0 + T], Hh[:, i, :], ACT.Square))
                p.dve.wait(t, nb["acct"])
                if i == 0:
                    u = p.dve.sig(tensor_copy(nb["acc"][:, :], nb["sq"][j][:, :]))
                else:
                    u = p.dve.sig(tensor_tensor(nb["acc"][:, :], nb["acc"][:, :],
                                                                 nb["sq"][j][:, :], ALU.add))
                nb["sqr"][j] = nb["acct"] = u
            yield
    p.tk["H"] = h
    if again:
        p.rstd(nb, N, 1.0 / D)
    yield


def run_beside(p, gen, n):
    if gen is not None:
        p.gens.append(gen)
    for _ in range(n):
        p.pump()
        p.ada(1)
    p.finish()


def second_block(p, HC, CX):
    act, dve, pe, PS, A, F = p.act, p.dve, p.pe, p.PS, p.A, p.F
    H = p.H
    Hh, Hl = HC
    while p.ada_at < 96:
        p.ada(1)
    p.mods(0)
    nb = p.norm_buffers("d", F + 16, 256)
    dve.wait(p.tk["H"])
    nc_ = p.norm_buffers("e", F, 256)
    for i in range(8):
        p.sq_add(nc_, CX[:, 2 * i:2 * i + 2, :], i == 0, [p.tk["cx"], p.tk["H"]])
    p.rstd(nc_, 256, 1.0 / D)
    for i in range(8):
        p.sq_add(nb, H[:, 2 * i:2 * i + 2, :], i == 0, [p.tk["H"]])
    p.rstd(nb, 256, 1.0 / D)
    act.wait(p.tk["hpe"], p.tk["G"])
    dve.wait(p.tk["hpe"], p.tk["G"], p.tk["cx"])
    mx = p.scaled(nb, tile_of(H), lambda k: p.coef(0, 0, 0, k), lambda k: p.shift(0, 0, k),
                  tile_of(Hh, 0, T), tile_of(Hl, 0, T), 0, T)
    mc = p.scaled(nc_, tile_of(CX), lambda k: p.coef(0, 0, 1, k), lambda k: p.shift(0, 1, k),
                  tile_of(Hh, T, 2 * T), tile_of(Hl, T, 2 * T), 0, T)

    def both(k):
        mx(k)
        return mc(k)

    X = Operand(tile_of(Hh), tile_of(Hl), NT, both, ahead=2)
    p.ada(8)
    layer0(p, X, HC)


def layer0(p, X, HC):
    act, dve, pe, PS, A, F = p.act, p.dve, p.pe, p.PS, p.A, p.F
    H = p.H
    N = 2 * T
    W = A["ev_w_in"]
    CC = p.sb("CC", [128, NT, N], F32, F + 96)
    AV = p.sb("AV", [128, 4, 256], F32, F)
    PL = p.sb("PL", [128, 2, N], F32, F + 4)
    MX = p.sb("MX", [128, 2, N], F32, F + 8)
    MM = p.sb("MM", [128, 4, 256], F32, F + 12)
    T1 = p.sb("T1", [128, 2, N], F32, F + 16)
    T2 = p.sb("T2", [128, 2, N], F32, F + 20)
    T3 = p.sb("T3", [128, 2, N], F32, F + 24)
    free = {"AV": None, "PL": None, "MX": None, "MM": None, "T1": None, "T2": None, "T3": None}
    p.ada_rate = ADA2

    def pooling(j, av, mm):
        for ct in range(2):
            pe.wait(av, mm, *p.bank_free[4 + ct])
            for w in range(2):
                for tk in range(2):
                    o = PS[4 + ct][:, w * 256:w * 256 + 256]
                    t = pe.sig(matmul(
                        o, AV[:, 2 * w + tk, ct * 128:ct * 128 + 128], MM[:, 2 * w + tk, :],
                        start=(w == 0 and tk == 0), stop=(tk == 1), skip_group_check=True))
        free["AV"] = free["MM"] = t
        yield
        for ct in range(2):
            act.wait(t, free["PL"])
            u = act.sig(activation(PL[:, ct, :], PS[4 + ct][:, :], ACT.Copy))
            p.bank_free[4 + ct] = [u]
        free["PLw"] = u
        yield

    def banks(s):
        return [PS[2 * s][:, :], PS[2 * s + 1][:, :]]

    xdone = None
    for j in range(4):
        if j == 0:
            s, t = p.group(W, 256 * j, 256, X, N, tm=True)
            xdone = t
            mm = p.load(MM[:, :, :], A["poolm"][j].rearrange("p (a b) -> p a b", a=4), "mm", [t])
        else:
            mm = p.load(MM[:, :, :], A["poolm"][j].rearrange("p (a b) -> p a b", a=4), "mm", [free["MM"]])
            s, t = p.group(W, 256 * j, 256, X, N, tm=True)
        act.wait(t, free["AV"])
        for i in range(2):
            u = act.sig(activation(AV[:, 2 * i:2 * i + 2, :], banks(s)[i], ACT.Copy))
        p.set_free[s] = [u]
        g = pooling(j, u, mm)
        p.gens.append(g)
        s, t = p.group(W, 2048 + 256 * j, 256, X, N)
        act.wait(t, free["T1"])
        for i in range(2):
            u = act.sig(activation(T1[:, i, :], banks(s)[i], ACT.Copy))
        p.set_free[s] = [u]
        bx = u
        p.finish(g)
        XP = Operand(tile_of(PL), None, 2, toks=[free["PLw"]] * 2)
        s, t = p.group(A["ev_pool_w"][j], 0, 256, XP, N, raw=True)
        free["PL"] = t
        dve.wait(t, free["MX"])
        for i in range(2):
            u = dve.sig(tensor_scalar(MX[:, i, :], banks(s)[i], p.v("pscale", 2 * j + i),
                                                            None, ALU.mult))
        p.set_free[s] = [u]
        mxw = u
        s, t = p.group(W, 4096 + 256 * j, 256, X, N)
        dve.wait(t, bx, free["T2"])
        for i in range(2):
            u = dve.sig(tensor_tensor(T2[:, i, :], banks(s)[i], T1[:, i, :], ALU.mult))
        p.set_free[s] = [u]
        act.wait(u, free["T3"])
        free["T1"] = u
        for i in range(2):
            m = 2 * j + i
            c = act.sig(activation(T3[:, i, :], T2[:, i, :], ACT.Identity,
                                                         scale=p.v("ecw", 8 + m), bias=p.v("ecb", m)))
        dve.wait(c, u)
        for n in range(2):
            for i in range(2):
                m = 2 * j + i
                a = T2[:, i, :].rearrange("p (w t) -> p w t", w=2)
                y = T3[:, i, :].rearrange("p (w t) -> p w t", w=2)
                if n == 0:
                    a, y, w = a[:, :, 0:T - 1], y[:, :, 1:T], p.v("ecw", m)
                else:
                    a, y, w = a[:, :, 1:T], y[:, :, 0:T - 1], p.v("ecw", 16 + m)
                u = dve.sig(scalar_tensor_tensor(y, a, w, y, ALU.mult, ALU.add))
            dve.wait(u)
        free["T2"] = u
        s, t = p.group(W, 3072 + 256 * j, 256, X, N)
        dve.wait(t, u)
        for i in range(2):
            u = dve.sig(tensor_tensor(T3[:, i, :], banks(s)[i], T3[:, i, :], ALU.mult))
        p.set_free[s] = [u]
        bb = u
        for c0, dst, src in ((5120, 8 + 2 * j, T3), (1024, 2 * j, MX)):
            s, t = p.group(W, c0 + 256 * j, 256, X, N)
            act.wait(t, free["T1"])
            for i in range(2):
                u = act.sig(activation(T1[:, i, :], banks(s)[i], ACT.Sigmoid))
            dve.wait(u, bb, mxw)
            for i in range(2):
                u = dve.sig(tensor_tensor(T1[:, i, :], banks(s)[i], T1[:, i, :], ALU.mult))
            p.set_free[s] = [u]
            dve.wait(u)
            if j == 0:
                dve.wait(xdone)
            u = dve.sig(tensor_tensor(CC[:, dst:dst + 2, :], T1[:, :, :],
                                                                    src[:, :, :], ALU.mult))
            free["T1"] = u
            free["T3" if src is T3 else "MX"] = u
    inproj = t
    p.finish()
    act.wait(inproj)
    dve.wait(inproj)
    CH = (p.HC[0], p.HC[1])
    X = late_split(p, tile_of(CC), tile_of(CH[0]), tile_of(CH[1]), NT, [u])
    X.ahead = 3
    Y = p.sb("Y0", [128, NT, N], F32, F + 96)
    CX = p.sb("CX2", [128, NT, T], F32, F)
    p.tk["cx"] = p.load(CX[:, :, :], A["ctxT"].rearrange("(k p) t -> p k t", p=128), "cx", [inproj, u])
    nb = p.norm_buffers("f", F + 16, 512)
    out_groups(p, A["ev_w_out"], X, Y, nb, N, 256)
    wout = (p.s_mm, len(p.chunks))
    while p.ada_at < 192 - 14:
        p.ada(1)
    p.dve.wait(p.tk["cx"])
    run_beside(p, residual(p, Y, nb, N, [(H, lambda k: p.coef(0, 1, 0, k), 0),
                                         (CX, lambda k: p.coef(0, 1, 1, k), T)], True), 14)
    p.mods(1)
    layer1(p, nb, CX, wout)


def layer1(p, nb, CX, wout):
    act, dve, pe, PS, A, F = p.act, p.dve, p.pe, p.PS, p.A, p.F
    H = p.H
    N = 2 * T
    XH, XL = p.HC
    act.wait(wout, p.tk["G"])
    dve.wait(wout, p.tk["G"])
    mx = p.scaled(nb, tile_of(H), lambda k: p.coef(1, 0, 0, k), lambda k: p.shift(1, 0, k),
                  tile_of(XH, 0, T), tile_of(XL, 0, T), 0, T)
    mc = p.scaled(nb, tile_of(CX), lambda k: p.coef(1, 0, 1, k), lambda k: p.shift(1, 1, k),
                  tile_of(XH, T, N), tile_of(XL, T, N), T, T)

    def both(k):
        mx(k)
        return mc(k)

    X = Operand(tile_of(XH), tile_of(XL), NT, both, ahead=2)
    XQ = Operand(tile_of(XH, 0, T), tile_of(XL, 0, T), NT)
    W = A["od_w_in"]
    V = p.sb("hV", [128, 4, 256], F32, F + 28)
    Q = p.sb("hQ", [128, 2, T], F32, F)
    G = p.sb("hG", [128, 2, T], F32, F + 2)
    Aa = p.sb("hA", [128, 2, N], F32, F + 4)
    B = p.sb("hB", [128, 2, N], F32, F + 8)
    C = p.sb("hC", [128, 2, N], F32, F + 12)
    KI = p.sb("hKI", [128, 2, T], F32, F + 16)
    QD = p.sb("hQD", [128, 2, T], F32, F + 18)
    ST = p.sb("hST", [128, 2, 4, 128], F32, F + 20)
    SC = p.sb("hSC", [128, 2, 2, 128], F32, F + 24)
    OT = p.sb("hOT", [128, 4, 128], F32, F + 26)
    OH, OL = halves(p, "O", NT, T, F + 96)
    rst = p.cst[:, CB["rst"]:CB["rst"] + 512]
    KD = B[:, :, :].rearrange("p h (a b) -> p h a b", a=4)
    f = {n: None for n in ("V", "Q", "G", "A", "B", "C", "KI", "QD", "ST", "SC", "OT", "O", "DEC", "OTr")}
    dec = p.DEC

    def direction(j, d, ztok, vtok, qtok):
        last = 63 if d == 0 else 0
        B16 = B[:, :, :].rearrange("p h (n c) -> p (h n) c", c=64)
        A16 = Aa[:, :, :].rearrange("p h (n c) -> p (h n) c", c=64)
        act.wait(ztok)
        for h in range(2):
            k = 2 * j + h
            t = act.sig(activation(
                Aa[:, h, :], Aa[:, h, :], ACT.Ln, scale=p.LB[:, 32 + 16 * d + k:33 + 16 * d + k],
                bias=p.LB[:, 16 * d + k:16 * d + k + 1]))
        yield
        dve.wait(t, f["B"], p.tk["rst"])
        for h in range(2):
            if d == 0:
                t = dve.sig(tensor_tensor_scan(B[:, h, :], rst, Aa[:, h, :], 0.0,
                                                                ALU.mult, ALU.add))
            else:
                t = dve.sig(tensor_tensor_scan(B[:, h, ::-1], rst, Aa[:, h, ::-1], 0.0,
                                                                ALU.mult, ALU.add))
        dve.wait(t)
        dl = dve.sig(tensor_tensor(A16, B16[:, :, last:last + 1].to_broadcast([128, 16, 64]), B16,
                                               ALU.subtract))
        yield
        act.wait(dl, f["KI"], f["QD"], f["DEC"])
        a = act.sig(activation(dec[:, 0:16], B16[:, :, last], ACT.Exp))
        a = act.sig(activation(Aa[:, :, :], Aa[:, :, :], ACT.Exp))
        a = act.sig(activation(KI[:, :, :], B[:, :, 0:T], ACT.Exp, scale=-1.0))
        a = act.sig(activation(QD[:, :, :], B[:, :, 0:T], ACT.Exp))
        yield
        dve.wait(a, qtok)
        for h in range(2):
            k = 2 * j + h
            om = p.LB[:, 32 + 16 * d + k:33 + 16 * d + k]
            u = dve.sig(scalar_tensor_tensor(Aa[:, h, :], C[:, h, :], om, Aa[:, h, :],
                                                                     ALU.mult, ALU.mult))
            u = dve.sig(scalar_tensor_tensor(KI[:, h, :], C[:, h, 0:T], om, KI[:, h, :],
                                                                     ALU.mult, ALU.mult))
        f["C"] = u
        u = dve.sig(tensor_tensor(QD[:, :, :], Q[:, :, :], QD[:, :, :], ALU.mult))
        f["Q"] = u
        yield
        order = [4, 5, 6, 7, 0, 1, 2, 3] if d == 0 else [7, 6, 5, 4, 3, 2, 1, 0]
        yield

        def turn(h):
            pe.wait(u, *p.bank_free[4])
            for i in range(4):
                t = pe.sig(transpose(PS[4][:, i * 128:i * 128 + 128], Aa[:, h, i * 128:i * 128 + 128],
                                     p.cst[:, 0:128]))
            f["A"] = t
            act.wait(t)
            kd = act.sig(activation(B[:, h, :], PS[4][:, :], ACT.Copy))
            p.bank_free[4] = [kd]
            return kd

        def ds(n):
            return PS[5 + n % 2][:, 128 * (n // 2):128 * (n // 2) + 128]

        def states(h, kd):
            pe.wait(kd, vtok, *p.bank_free[5], *p.bank_free[6])
            for n in order[:7]:
                r = 64 * (n % 2)
                pe.run(matmul(ds(n), KD[r:r + 64, h, n // 2, :], V[r:r + 64, n // 2, h * 128:h * 128 + 128],
                              start=True, stop=True, skip_group_check=True))
            for i in range(2):
                c = 128 * i
                t = pe.sig(matmul(PS[4][:, c:c + 128], KI[:, h, c:c + 128], QD[:, h, c:c + 128],
                                  start=True, stop=True, skip_group_check=True))
            f["B"] = f["KI"] = t
            dve.wait(t, f["SC"], f["ST"])
            sc = dve.sig(tensor_tensor(
                SC[:, h, :, :].bitcast(I32), PS[4][:, 0:256].bitcast(I32).rearrange("p (a b) -> p a b", a=2),
                p.hgm[:, 128 * d:128 * d + 128].unsqueeze(1).to_broadcast([128, 2, 128]), ALU.bitwise_and))
            p.bank_free[4] = [sc]
            s0 = order[4]
            u = dve.sig(tensor_copy(ST[:, h, s0, :], ds(order[0])))
            for i in range(1, 7):
                n = order[i]
                frm, to = (s0, s0) if i < 4 else (n, order[i + 1])
                dve.wait(u)
                u = dve.sig(scalar_tensor_tensor(
                    ST[:, h, to, :], ST[:, h, frm, :], dec[:, 8 * h + n:8 * h + n + 1], ds(n), ALU.mult, ALU.add))
            p.bank_free[5] = p.bank_free[6] = [u]
            f["DEC"] = u
            return u

        def outputs(h, st):
            pe.wait(st)
            if d == 0 and h == 0:
                pe.wait(*p.bank_free[7])
            for n in range(4):
                r, c = 64 * (n % 2), 256 * h + 128 * (n // 2)
                pe.run(matmul(PS[7][r:r + 64, c:c + 128], QD[:, h, n * 64:n * 64 + 64], ST[:, h, n, :],
                              start=(d == 0 and h == 0 and n < 2), stop=False, skip_group_check=True))
            for i in range(2):
                c = 256 * h + 128 * i
                t = pe.sig(matmul(PS[7][:, c:c + 128], SC[:, h, i, :], V[:, i, h * 128:h * 128 + 128],
                                  start=False, stop=(d == 1), skip_group_check=True))
            f["QD"] = f["ST"] = f["SC"] = f["V"] = f["O"] = t

        kd = turn(0)
        yield
        st0 = states(0, kd)
        yield
        kd = turn(1)
        yield
        outputs(0, st0)
        st1 = states(1, kd)
        yield
        yield
        outputs(1, st1)
        yield

    def readout(j, gtok):
        act.wait(f["O"], f["OTr"])
        for i in range(4):
            t = act.sig(activation(OT[:, i, :], PS[7][:, 128 * i:128 * i + 128], ACT.Square,
                                   accum_out=p.SM[:, i:i + 1]))
        dve.wait(t)
        t = dve.sig(tensor_scalar(p.SM[:, 4:8], p.SM[:, 0:4], 1.0 / 128, EPS, ALU.mult, ALU.add))
        act.wait(t)
        t = act.sig(activation(p.SM[:, 4:8], p.SM[:, 4:8], ACT.Sqrt))
        dve.wait(t)
        t = dve.sig(reciprocal(p.SM[:, 4:8], p.SM[:, 4:8]))
        yield
        yield
        act.wait(t)
        for i in range(4):
            t = act.sig(activation(OT[:, i, :], PS[7][:, 128 * i:128 * i + 128], ACT.Copy,
                                   scale=p.SM[:, 4 + i:5 + i]))
        p.bank_free[7] = [t]
        yield
        pe.wait(t, *p.bank_free[4])
        for i in range(4):
            t = pe.sig(transpose(PS[4][:, 128 * i:128 * i + 128], OT[:, i, :], p.cst[:, 0:128]))
        dve.wait(t, gtok)
        for h in range(2):
            t = dve.sig(scalar_tensor_tensor(G[:, h, :], PS[4][:, 256 * h:256 * h + 256], p.v("onorm", 2 * j + h),
                                             G[:, h, :], ALU.mult, ALU.mult))
        p.bank_free[4] = [t]
        f["OTr"] = t
        act.wait(t)
        h_ = act.sig(activation(OH[:, 2 * j:2 * j + 2, :], G[:, :, :], ACT.Copy))
        dve.wait(h_, t)
        t = dve.sig(tensor_tensor(OL[:, 2 * j:2 * j + 2, :], G[:, :, :],
                                  OH[:, 2 * j:2 * j + 2, :].bitcast(F32), ALU.subtract))
        f["G"] = t
        otoks.extend([t, t])
        yield

    otoks = []
    p.serial = True

    def values(j):
        s, t = p.group(W, 4096 + 256 * j, 256, X, N, tm=True)
        p.finish(*works)
        act.wait(t, f["V"])
        for i in range(2):
            u = act.sig(activation(V[:, 2 * i:2 * i + 2, :], PS[2 * s + i][:, :], ACT.Copy))
        p.set_free[s] = [u]
        return u, t

    def queries(j):
        s, t = p.group(W, 6144 + 256 * j, 256, XQ, T)
        act.wait(t, f["Q"])
        u = act.sig(activation(Q[:, :, :], PS[2 * s][:, :], ACT.Copy))
        p.set_free[s] = [u]
        return u

    def forget(j, d):
        s, t = p.group(W, 2048 * d + 256 * j, 256, X, N)
        p.finish(*works)
        act.wait(t, f["A"], f["C"])
        for i in range(2):
            act.run(activation(C[:, i, :], PS[2 * s + i][:, :], ACT.Sigmoid, scale=-1.0))
            u = act.sig(activation(Aa[:, i, :], PS[2 * s + i][:, :], ACT.Sigmoid))
        p.set_free[s] = [u]
        return u, t

    works = []
    for j in range(8):
        if j == 0:
            vt, XQ.toks = values(j)[0], X.toks
            qt = queries(j)
        else:
            qt = queries(j)
            vt = values(j)[0]
        zt = forget(j, 0)[0]
        works = [direction(j, 0, zt, vt, qt)]
        p.gens += works
        s, t = p.group(W, 8192 + 256 * j, 256, XQ, T)
        act.wait(t, f["G"])
        u = act.sig(activation(G[:, :, :], PS[2 * s][:, :], ACT.Sigmoid))
        dve.wait(u)
        gt = dve.sig(tensor_tensor(G[:, :, :], PS[2 * s][:, :], G[:, :, :], ALU.mult))
        p.set_free[s] = [gt]
        zt, t = forget(j, 1)
        works = [direction(j, 1, zt, vt, qt)]
        p.gens += works + [readout(j, gt)]
    inproj = t
    p.finish()
    p.serial = False
    X = Operand(tile_of(OH), tile_of(OL), NT, toks=otoks)
    Y = p.sb("Y1", [128, NT, T], F32, F + 32)
    nb = p.norm_buffers("g", F + 48, 256)
    act.wait(inproj, otoks[-1])
    dve.wait(inproj)
    out_groups(p, A["od_w_out"], X, Y, nb, T, 512)
    p.gens = [residual(p, Y, nb, T, [(H, lambda k: p.coef(1, 1, 0, k), 0)], False)]
    p.finish()
    p.load(A["out"].rearrange("(k p) t -> p k t", p=128), H[:, :, :], "out", [p.tk["H"]])


ADA1 = 0.26
ADA2 = 0.75


def build(nc, A):
    p = Program(nc, A)
    p.tk = {}
    act, dve, pe, pool = p.act, p.dve, p.pe, p.pool
    p.tk["x"] = p.load(p.H[:, :, :], A["xT"].rearrange("(k p) t -> p k t", p=128), "x")
    p.tk["vec"] = p.load(p.vec[:, :], A["vec"], "vec")
    p.tk["c0"] = p.load(p.cst[:, :], A["cst"][:, 0:NCB], "cst")
    p.tk["hgm"] = p.load(p.hgm[:, :], A["hgm"], "hgm")
    p.tk["ones"] = dve.sig(memset(p.ones[:, :], 1.0))
    for lane in (act, dve, pe):
        lane.wait(p.tk["vec"], p.tk["c0"], p.tk["hgm"])
    cv = p.v("c", 0, 32)
    t = act.sig(activation(p.S[:, :], cv, ACT.Sigmoid))
    dve.wait(t)
    p.tk["S"] = dve.sig(tensor_tensor(p.S[:, :], p.S[:, :], cv, ALU.mult))
    L = [p.vec[:, VEC["lb"]:VEC["lb"] + 96].rearrange("p (d i k) -> p d i k", d=2, i=3)[:, :, i, :] for i in range(3)]
    m = p.SM[:, 0:32].rearrange("p (d k) -> p d k", d=2)
    lb = p.LB[:, 0:32].rearrange("p (d k) -> p d k", d=2)
    om = p.LB[:, 32:64].rearrange("p (d k) -> p d k", d=2)
    t = dve.sig(tensor_tensor(m, L[0], L[1], ALU.max))
    dve.wait(t)
    t = dve.sig(tensor_tensor(m, m, L[2], ALU.max))
    dve.wait(t)
    for i in range(3):
        t = dve.sig(tensor_tensor(L[i], L[i], m, ALU.subtract))
    act.wait(t)
    for i in range(3):
        t = act.sig(activation(L[i], L[i], ACT.Exp))
    dve.wait(t)
    t = dve.sig(tensor_tensor(lb, L[0], L[1], ALU.add))
    dve.wait(t)
    t = dve.sig(tensor_tensor(m, lb, L[2], ALU.add))
    dve.wait(t)
    t = dve.sig(reciprocal(m, m))
    dve.wait(t)
    t = dve.sig(tensor_tensor(lb, lb, m, ALU.mult))
    dve.wait(t)
    p.tk["lb"] = dve.sig(tensor_scalar(om, lb, -1.0, 1.0, ALU.mult, ALU.add))
    act.wait(p.tk["lb"])
    HC, CX = first_block(p)
    p.HC = HC
    second_block(p, HC, CX)
    p.play_stream()
    pool.wait((p.s_ld["out"][0], p.s_ld["out"][1]))
    with nc.Block() as block:
        @block.sync
        def _(e):
            p.sp.play(e)

        @block.scalar
        def _(e):
            act.play(e)

        @block.vector
        def _(e):
            dve.play(e)

        @block.tensor
        def _(e):
            pe.play(e)

        @block.gpsimd
        def _(e):
            pool.play(e)


def constants():
    f = np.float32
    q = np.arange(T)[:, None]
    k = np.arange(T)[None, :]
    bias = np.full((3, 2, 128, 256), -1e38, f)
    for g, (win, dil) in enumerate(((128, 1), (512, 4), (2048, 16))):
        ok = (k <= q) & ((q - k) % dil == 0) & ((q - k) // dil <= win // dil)
        bias[g] = np.where(ok, -(q - k), -1e38).astype(f).reshape(2, 128, 256)
    bias = np.ascontiguousarray(bias.transpose(2, 0, 1, 3).reshape(128, -1))
    i = np.arange(128)
    cst = np.zeros((128, 1152), f)
    cst[:, 0:128] = np.eye(128)
    cst[:, 128:256] = i[:, None] > i[None, :]
    strict = i[:, None] < i[None, :]
    cst[:, 256:384] = strict
    cst[:, 384:512] = 1
    cst[:, 512:640] = strict
    cst[:, 640:1152] = (np.arange(512) % 64 != 0)[None]
    s, c = np.arange(128)[:, None], np.arange(128)[None, :]
    near = s // 64 == c // 64
    hgm = np.concatenate([near & (s <= c), near & (s >= c)], axis=1)
    hgm = np.where(hgm, -1, 0).astype(np.int32)

    def mean(n, w):
        t = np.arange(n)
        lo, hi = np.maximum(t - w // 2, 0), np.minimum(t + w // 2 - 1, n - 1)
        m = (t[None, :] >= lo[:, None]) & (t[None, :] <= hi[:, None])
        return m / (hi - lo + 1)[:, None]

    pool = np.zeros((4, 128, 4, 256), f)
    for g, w in enumerate((2, 4, 8, 16)):
        grid = np.kron(mean(4, w), mean(64, w)) - np.eye(256)
        line = mean(256, w) - np.eye(256)
        for n, m in enumerate((grid, line)):
            pool[g, :, 2 * n:2 * n + 2, :] = m.T.reshape(2, 128, 256).transpose(1, 0, 2)
    return {"bias": bias, "cst": cst, "hgm": hgm, "poolm": pool.reshape(4, 128, 1024)}


def kernel(**inputs):
    import concourse.bacc as bacc
    from concourse.bass_utils import run_bass_kernel_spmd as run

    a = {n: np.asarray(v) for n, v in inputs.items()}

    def col(v):
        v = v.reshape(-1, 128) if v.ndim == 1 else v.reshape(v.shape[0] * (v.shape[1] // 128), 128)
        return v.T

    lb = a["lb_logits_2"].reshape(2 * 3 * 16, 128).T
    cc = np.stack([a["c_2"][0].reshape(16, 128), a["c_ctx_2"].reshape(16, 128)], axis=1).reshape(32, 128).T
    parts = [col(a["g_mix_pre"][0]), col(a["g_mix_post"][0]), col(a["g_ffn_pre"][0]), col(a["g_ffn_post"][0]),
             col(a["pre_g_2"][0]), col(a["pre_g_2"][1]), col(a["post_g_2"][0]), col(a["post_g_2"][1]),
             col(a["ev_pool_scale_2"][0]), col(a["ev_conv_w_2"][0]), col(a["ev_conv_b_2"][0]),
             col(a["conv_w"][0]), col(a["conv_b"][0]), col(a["od_onorm_g_2"][0]), lb, col(a["ada_b_2"]), cc]
    arrays = {
        "xT": a["x"][0].T, "ctxT": a["ctx_2"][0].T, "pT": a["p"][0, 0].T,
        "vec": np.concatenate(parts, axis=1),
        "w_in": a["w_in"][0], "w_ba": a["w_branch_a"][0], "w_bb": a["w_branch_b"][0], "w_out": a["w_out"][0],
        "w_up": a["w_up"][0], "w_down": a["w_down"][0], "w_ple_in": a["w_ple_in"][0],
        "w_ple_gate": a["w_ple_gate"][0], "ada_w": a["ada_w_2"], "ev_w_in": a["ev_w_in_2"][0],
        "ev_pool_w": a["ev_pool_w_2"][0], "ev_w_out": a["ev_w_out_2"][0], "od_w_in": a["od_w_in_2"][0],
        "od_w_out": a["od_w_out_2"][0],
    }
    arrays.update(constants())
    arrays = {n: np.ascontiguousarray(v) for n, v in arrays.items()}
    nc = bacc.Bacc("TRN2", target_bir_lowering=False, num_devices=1)
    A = {n: nc.dram_tensor(f"in_{n}", v.shape, mybir.dt.from_np(v.dtype), kind="ExternalInput").ap()
         for n, v in arrays.items()}
    A["out"] = nc.dram_tensor("out_0", (D, T), F32, kind="ExternalOutput").ap()
    build(nc, A)
    r = run(nc, [{f"in_{n}": v for n, v in arrays.items()}], core_ids=[0])
    return r.results[0]["out_0"].T.reshape(1, T, D)
```

```python
import numpy as np

import concourse.bass as bass
from concourse import mybir

F32 = mybir.dt.float32
F32R = mybir.dt.float32r
I32 = mybir.dt.int32
ALU = mybir.AluOpType
ACT = mybir.ActivationFunctionType
AX = mybir.AxisListType

D = 2048
T = 256
NT = D // 128
DFF = 5632
NF = DFF // 128
EPS = 1e-6
QS = 1.0 / float(np.sqrt(128.0))
RING, SPLIT, AHEAD = 5, 4, 3
ADA_GROUPS = [(l, g) for l in range(2) for g in range(12)]

VEC = {}


def _place():
    at = 0
    for name, n in (("g_mix_pre", 16), ("g_mix_post", 16), ("g_ffn_pre", 16), ("g_ffn_post", 16),
                    ("pre0", 16), ("pre1", 16), ("post0", 16), ("post1", 16), ("pscale", 8),
                    ("ecw", 24), ("ecb", 8), ("cw", 264), ("cb", 88), ("onorm", 16),
                    ("lb", 96), ("adab", 96), ("c", 32)):
        VEC[name] = at
        at += n
    return at


NVEC = _place()
CB = {"ident": 0, "tri": 128, "ms": 256, "rst": 128}
NCB = 640


def matmul(*a, **k):
    return lambda e: e.matmul(*a, **k)


def transpose(*a, **k):
    return lambda e: e.transpose(*a, **k)


def activation(*a, **k):
    return lambda e: e.activation(*a, **k)


def tensor_tensor(*a, **k):
    return lambda e: e.tensor_tensor(*a, **k)


def scalar_tensor_tensor(*a, **k):
    return lambda e: e.scalar_tensor_tensor(*a, **k)


def tensor_scalar(*a, **k):
    return lambda e: e.tensor_scalar(*a, **k)


def tensor_copy(*a, **k):
    return lambda e: e.tensor_copy(*a, **k)


def tensor_reduce(*a, **k):
    return lambda e: e.tensor_reduce(*a, **k)


def tensor_tensor_scan(*a, **k):
    return lambda e: e.tensor_tensor_scan(*a, **k)


def reciprocal(*a, **k):
    return lambda e: e.reciprocal(*a, **k)


def memset(*a, **k):
    return lambda e: e.memset(*a, **k)


def dma_start(*a, **k):
    return lambda e: e.dma_start(*a, **k)


class Lane:

    def __init__(self, sem):
        self.sem, self.n, self.items = sem, 0, []

    def wait(self, *toks):
        self.items += [("wait", t) for t in toks if t is not None]

    def run(self, fn):
        self.items.append(("run", fn))

    def sig(self, fn):
        self.n += 1
        self.items.append(("sig", fn, self.sem, 1))
        return (self.sem, self.n)

    def sig_on(self, fn, sem, by):
        self.items.append(("sig", fn, sem, by))

    def mark(self):
        sub = []
        self.items.append(("sub", sub))
        return sub

    def play(self, eng, items=None, seen=None):
        items = self.items if items is None else items
        seen = {} if seen is None else seen
        for it in items:
            if it[0] == "wait":
                sem, n = it[1]
                if seen.get(id(sem), 0) < n:
                    eng.wait_ge(sem, n)
                    seen[id(sem)] = n
            elif it[0] == "run":
                it[1](eng)
            elif it[0] == "sig":
                it[1](eng).then_inc(it[2], it[3])
            else:
                self.play(eng, it[1], seen)


class Operand:

    def __init__(self, hi, lo, n, make=None, toks=None, ahead=0):
        self.hi, self.lo, self.n, self.make, self.ahead = hi, lo, n, make, ahead
        self.toks = list(toks or [])

    def need(self, k):
        if self.make is not None:
            while len(self.toks) <= min(k + self.ahead, self.n - 1):
                self.toks.append(self.make(len(self.toks)))
        return self.toks[k] if k < len(self.toks) else None


class Program:
    def __init__(self, nc, A):
        self.nc, self.A = nc, A
        s = nc.alloc_semaphore
        self.act, self.dve, self.pe = Lane(s("act")), Lane(s("dve")), Lane(s("pe"))
        self.pool, self.sp = Lane(s("pool")), Lane(s("sp"))
        self.last = Lane(None)
        self.s_raw = [s(f"raw{i}") for i in range(RING)]
        self.s_hi, self.s_lo, self.s_lop, self.s_mm = s("hi"), s("lo"), s("lop"), s("mm")
        self.pool_split = 0
        self.nlo = {}
        self.s_ld = {}
        self.base = (nc.sbuf_base + 31) // 32 * 32
        self.names = set()
        self.chunks = []
        self.marks = []
        self.nsplit = 0
        self.split_pe = []
        self.set_at = 0
        self.set_free = [[], []]
        self.bank_free = {b: [] for b in range(4, 8)}
        self.gens = []
        self.serial = False
        self.early = []
        self.split_at = []
        self.ada_at = 0
        self.pending = None
        self.ada_rate = 0.0
        self.ada_due = 0.0
        self.PS = [nc.alloc_psum_tensor(f"ps{i}", [128, 512], F32) for i in range(8)]
        at = 0
        self.raw = [self.sb(f"raw_{i}", [128, 1024], F32, at + 4 * i) for i in range(RING)]
        at += 4 * RING
        self.whi = [self.sb(f"whi{i}", [128, 1024], F32R, at + 4 * i) for i in range(SPLIT)]
        at += 4 * SPLIT
        self.wlo = [self.sb(f"wlo{i}", [128, 1024], F32R, at + 4 * i) for i in range(SPLIT)]
        at += 4 * SPLIT
        self.vec = self.sb("vec", [128, NVEC], F32, at)
        at += 3
        self.cst = self.sb("cst", [128, NCB], F32, at)
        at += 2.5
        self.R = self.sb("R", [128, 512], F32, at)
        at += 2
        self.ones = self.sb("ones", [128, 128], F32, at)
        self.hgm = self.sb("hgm", [128, 256], I32, at + 0.5)
        at += 1.5
        self.M = self.sb("M", [128, 2 * 2 * 48], F32, at)
        self.G = self.sb("G", [128, 128], F32, at + 0.75)
        self.S = self.sb("S", [128, 32], F32, at + 1.25)
        self.LB = self.sb("LB", [128, 64], F32, at + 1.375)
        self.DEC = self.sb("DEC", [128, 16], F32, at + 1.625)
        self.SM = self.sb("SM", [128, 64], F32, at + 1.75)
        self.eps = self.SM[:, 25:26]
        at += 2
        self.P0 = at
        self.H = self.sb("H", [128, NT, T], F32, at)
        self.F = at + 16

    def sb(self, name, shape, dt, kb):
        off = self.base + int(round(kb * 1024))
        return self.nc.alloc_sbuf_tensor_at(name, shape, dt, offset=off)

    def v(self, name, k=0, n=1):
        a = VEC[name] + k
        return self.vec[:, a:a + n]

    def load(self, dst, src, name, after=(), lane=None):
        lane = lane or self.pool
        sem = self.s_ld.get(name)
        if sem is None:
            sem = [self.nc.alloc_semaphore(f"ld_{name}"), 0]
            self.s_ld[name] = sem
        lane.wait(*after)
        sem[1] += 16
        lane.sig_on(dma_start(dst, src), sem[0], 16)
        return (sem[0], sem[1])

    def chunk(self, src, kt, cols, split):
        c = len(self.chunks)
        slot, use = c % RING, c // RING
        n = kt * cols
        raw = self.raw[slot][:, 0:n]
        landed = (self.s_raw[slot], 16 * (use + 1))
        self.marks.append((self.act.mark(), self.dve.mark(), self.pool.mark()))
        ch = {"src": src, "dst": raw.rearrange("p (k c) -> p k c", k=kt)}
        if split:
            i = self.nsplit
            self.nsplit += 1
            hi, lo = self.whi[i % SPLIT][:, 0:n], self.wlo[i % SPLIT][:, 0:n]
            self.split_at.append(c)
            at = self.split_at[i - AHEAD] if i >= AHEAD else 0
            ma, md, mp = self.early[c] if c < len(self.early) else self.marks[max(at, c - RING + 1)]
            done = self.s_lo
            if self.pool_split and i % self.pool_split == 0:
                md, done = mp, self.s_lop
            self.nlo[id(done)] = self.nlo.get(id(done), 0) + 1
            done = (done, self.nlo[id(done)])
            ma.append(("wait", landed))
            if i >= SPLIT:
                ma.append(("wait", self.split_pe[i - SPLIT]))
            ma.append(("sig", activation(hi, raw, ACT.Copy), self.s_hi, 1))
            md.append(("wait", landed))
            md.append(("wait", (self.s_hi, i + 1)))
            if i >= SPLIT:
                md.append(("wait", self.split_pe[i - SPLIT]))
            md.append(("sig", tensor_tensor(lo, raw, hi.bitcast(F32), ALU.subtract), done[0], 1))
            ch["ready"] = done
            ch["hi"] = hi.rearrange("p (k c) -> p k c", k=kt)
            ch["lo"] = lo.rearrange("p (k c) -> p k c", k=kt)
            ch["free"] = done
            self.split_pe.append((self.s_mm, c + 1))
        else:
            ch["ready"] = landed
            ch["hi"] = ch["dst"]
            ch["free"] = (self.s_mm, c + 1)
        self.chunks.append(ch)
        return ch

    def play_stream(self):
        for c, ch in enumerate(self.chunks):
            if c >= RING:
                self.sp.wait(self.chunks[c - RING]["free"])
            self.sp.sig_on(dma_start(ch["dst"], ch["src"]), self.s_raw[c % RING], 16)

    def pump(self):
        for g in self.gens[0:1] if self.serial else list(self.gens):
            if next(g, "end") == "end":
                self.gens.remove(g)

    def finish(self, *gens):
        for g in gens or list(self.gens):
            while g in self.gens:
                h = self.gens[0] if self.serial else g
                if next(h, "end") == "end":
                    self.gens.remove(h)

    def tiles(self, s, width):
        per = 512 // width
        return lambda i: self.PS[2 * s + i // per][:, (i % per) * width:(i % per + 1) * width]

    def group(self, W, c0, cols, X, N, tm=False, raw=False, quiet=False, part=None, s=None):
        K = X.n
        kt = min(K, 1024 // cols)
        if s is None:
            s = self.set_at % 2
            self.set_at += 1
        width = cols if tm else N
        out, per = self.tiles(s, width), 512 // width
        count = N // 128 if tm else cols // 128
        for j in range(*(part or (0, K // kt))):
            src = W[j * kt * 128:(j + 1) * kt * 128, c0:c0 + cols].rearrange("(k p) c -> p k c", p=128)
            for k in range(j * kt, (j + 1) * kt):
                X.need(k)
            c = len(self.chunks)
            ch = self.chunk(src, kt, cols, not raw)
            self.pump()
            self.pe.wait(ch["ready"])
            if j == 0:
                self.pe.wait(*self.set_free[s])
            for k in range(kt):
                kk = j * kt + k
                if self.serial and N == 512 and 2 * k == kt:
                    self.pump()
                self.pe.wait(X.need(kk))
                for i in range(count):
                    first = kk == 0 and i % per == 0
                    if tm:
                        cut = slice(i * 128, (i + 1) * 128)
                        xs = [X.hi(kk)[:, cut]] + ([] if raw else [X.lo(kk)[:, cut]])
                        ws = [ch["hi"][:, k, :]] + ([] if raw else [ch["lo"][:, k, :]])
                        terms = [(xs[0], ws[0])] + ([] if raw else [(xs[1], ws[0]), (xs[0], ws[1])])
                    else:
                        cut = slice(i * 128, (i + 1) * 128)
                        xs = [X.hi(kk)] + ([] if raw else [X.lo(kk)])
                        ws = [ch["hi"][:, k, cut]] + ([] if raw else [ch["lo"][:, k, cut]])
                        terms = [(ws[0], xs[0])] + ([] if raw else [(ws[1], xs[0]), (ws[0], xs[1])])
                    for t, (a, b) in enumerate(terms):
                        last = kk == K - 1 and t == len(terms) - 1
                        o = out(i)
                        fn = matmul(o, a, b, start=first and t == 0, stop=last, skip_group_check=True)
                        if k == kt - 1 and i == count - 1 and t == len(terms) - 1:
                            self.pe.sig_on(fn, self.s_mm, 1)
                        else:
                            self.pe.run(fn)
            if not quiet:
                self.ada_due += self.ada_rate
                while self.ada_due >= 1:
                    self.ada_due -= 1
                    self.ada(1)
        return s, (self.s_mm, c + 1)

    def ada(self, n):
        for _ in range(n):
            if self.ada_at >= 8 * len(ADA_GROUPS):
                return
            g, j = divmod(self.ada_at, 8)
            self.ada_at += 1
            l, m = ADA_GROUPS[g]
            bank = 6 + g % 2
            W = self.A["ada_w"][l]
            src = W[j * 256:(j + 1) * 256, m * 512:(m + 1) * 512].rearrange("(k p) c -> p k c", p=128)
            c = len(self.chunks)
            ch = self.chunk(src, 2, 512, False)
            self.pe.wait(ch["ready"])
            if j == 0:
                self.pe.wait(*self.bank_free[bank])
                self.pe.wait(self.tk["S"])
            for k in range(2):
                n = 2 * j + k
                r = 32 * (n % 4)
                fn = matmul(self.PS[bank][r:r + 2, :], self.S[:, 2 * n:2 * n + 2], ch["hi"][:, k, :],
                            start=n < 4, stop=n >= 12, skip_group_check=True)
                if k == 1:
                    self.pe.sig_on(fn, self.s_mm, 1)
                else:
                    self.pe.run(fn)
            if j == 7:
                self.act.wait((self.s_mm, c + 1), self.tk.get("Rfree"))
                t = self.act.sig(activation(self.R[:, :], self.PS[bank][:, :], ACT.Copy))
                self.bank_free[bank] = [t]
                self.pending = (g, t)
            elif j == 1 and self.pending:
                self.ada_end()

    def ada_end(self):
        g, t = self.pending
        self.pending = None
        l, m = ADA_GROUPS[g]
        bank = 6 + g % 2
        self.pe.wait(t)
        for i in range(4):
            u = self.pe.sig(transpose(self.PS[bank][:, 128 * i:128 * i + 128], self.R[:, 128 * i:128 * i + 128],
                                      self.cst[:, 0:128]))
        self.tk["Rfree"] = u
        self.dve.wait(u)
        for w in range(2):
            a = (l * 2 + w) * 48 + 4 * m
            v = self.PS[bank][:, :].rearrange("p (i j q) -> p i q j", i=4, j=4)[:, :, w, :]
            tok = self.dve.sig(tensor_reduce(self.M[:, a:a + 4], v, AX.X, ALU.add))
        self.bank_free[bank] = [tok]
        self.dve.wait(tok)
        for w in range(2):
            a = (l * 2 + w) * 48 + 4 * m
            tok = self.dve.sig(tensor_tensor(self.M[:, a:a + 4], self.M[:, a:a + 4],
                                             self.v("adab", l * 48 + 4 * m, 4), ALU.add))
        self.tk["M"] = tok

    def mods(self, l):
        if self.pending:
            self.ada_end()
        d, g0 = self.dve, 64 * l
        d.wait(self.tk["M"])
        for w in range(2):
            a = (l * 2 + w) * 48
            t = d.sig(scalar_tensor_tensor(
                self.G[:, g0 + 16 * w:g0 + 16 * w + 16], self.M[:, a + 16:a + 32], 1.0,
                self.v(f"pre{l}", 0, 16), ALU.add, ALU.mult))
            t = d.sig(tensor_tensor(
                self.G[:, g0 + 32 + 16 * w:g0 + 48 + 16 * w], self.M[:, a + 32:a + 48],
                self.v(f"post{l}", 0, 16), ALU.mult))
        self.tk["G"] = t

    def shift(self, l, w, k):
        a = (l * 2 + w) * 48 + k
        return self.M[:, a:a + 1]

    def coef(self, l, what, w, k):
        a = 64 * l + 32 * what + 16 * w + k
        return self.G[:, a:a + 1]

    def norm_buffers(self, tag, kb, N=256, bank=5, rs=None, share=None, acc=True):
        if share is None:
            b = {"sq": [self.sb(f"sq{tag}{i}", [128, 512], F32, kb + 2 * i) for i in range(2)],
                 "t": [self.sb(f"t{tag}{i}", [128, 256], F32, kb + 4 + i) for i in range(3)],
                 "sqr": [None, None], "tfree": {}, "n": [0]}
        else:
            b = {n: share[n] for n in ("sq", "t", "sqr", "tfree", "n")}
        if acc:
            b["acc"] = self.sb(f"acc{tag}", [128, 512], F32, kb + 7)
        b["rs"] = self.sb(f"rs{tag}", [128, N], F32, kb + 9 if rs is None else rs)
        b.update(N=N, bank=bank, acct=None, begun=False)
        return b

    def add_up(self, b, sq, after):
        self.pe.wait(after, self.tk["ones"])
        if not b["begun"]:
            self.pe.wait(*self.bank_free[b["bank"]])
        for a in range(0, 512, b["N"]):
            t = self.pe.sig(matmul(self.PS[b["bank"]][0:1, 0:b["N"]], self.ones[:, 0:1], sq[:, a:a + b["N"]],
                                   start=not b["begun"], stop=True, skip_group_check=True))
            b["begun"] = True
        return t

    def sq_add(self, b, src, after=(), direct=False):
        i = b["n"][0] % 2
        b["n"][0] += 1
        self.act.wait(*after)
        self.act.wait(b["sqr"][i])
        t = self.act.sig(activation(b["sq"][i][:, :], src, ACT.Square))
        if direct:
            b["sqr"][i] = self.add_up(b, b["sq"][i], t)
            return t
        self.dve.wait(t)
        self.dve.wait(b["acct"])
        if b["acct"] is None:
            u = self.dve.sig(tensor_copy(b["acc"][:, :], b["sq"][i][:, :]))
        else:
            u = self.dve.sig(tensor_tensor(b["acc"][:, :], b["acc"][:, :], b["sq"][i][:, :], ALU.add))
        b["sqr"][i] = b["acct"] = u
        return t

    def rstd(self, b):
        for _ in self.rstd_steps(b):
            pass

    def rstd_steps(self, b):
        n, bank = b["N"] // 128, b["bank"]
        root = self.SM[:, 8 * (bank - 4):8 * (bank - 4) + n]
        self.act.run(activation(self.SM[:, 24:25], self.ones[:, 0:1], ACT.Sqrt))
        if b["acct"] is not None:
            self.add_up(b, b["acc"], b["acct"])
        self.act.wait((self.pe.sem, self.pe.n), self.tk["ones"], b["sqr"][1])
        row = b["sq"][1]
        t = self.act.sig(activation(row[0:1, 0:b["N"]], self.PS[bank][0:1, 0:b["N"]], ACT.Sqrt, scale=1.0 / D,
                                    bias=self.eps[0:1, :]))
        yield
        first = not self.chunks
        if first:
            ma = self.act.mark()
        self.pe.wait(t)
        for i in range(n):
            t = self.pe.sig(matmul(self.PS[bank][:, i:i + 1], row[0:1, 128 * i:128 * i + 128], self.ones[0:1, 0:1],
                                   start=(i == 0), stop=True, skip_group_check=True))
        b["sqr"][1] = t
        self.dve.wait(t)
        t = self.dve.sig(reciprocal(root, self.PS[bank][:, 0:n]))
        self.dve.wait(t, b["sqr"][0])
        d = b["sq"][0]
        for i in range(n):
            t = self.dve.sig(tensor_scalar(d[:, 128 * i:128 * i + 128], self.cst[:, 0:128], root[:, i:i + 1], None,
                                           ALU.mult))
        if first:
            md = self.dve.mark()
            self.early = [(ma, md, None)] * 2
        yield
        self.pe.wait(t)
        for i in range(n):
            t = self.pe.sig(matmul(self.PS[bank][:, 128 * i:128 * i + 128], self.ones[:, :],
                                   d[:, 128 * i:128 * i + 128], start=(i == 0), stop=True, skip_group_check=True))
        b["sqr"][0] = t
        self.act.wait(t)
        self.act.wait(*b["tfree"].values())
        t = self.act.sig(activation(b["rs"][:, :], self.PS[bank][:, 0:b["N"]], ACT.Copy))
        self.bank_free[bank] = [t]
        self.dve.wait(t)
        b["rst"] = t
        b["acct"], b["begun"] = None, False
        return t

    def scaled(self, b, src, coef, shift, hi, lo):
        begun = []

        def start(k):
            t = b["t"][k % 3][:, :]
            self.dve.wait(b["tfree"].get(k % 3))
            d = self.dve.sig(scalar_tensor_tensor(t, src(k), coef(k), b["rs"][:, :], ALU.mult, ALU.mult))
            self.act.wait(d)
            if shift is None:
                h = self.act.sig(activation(hi(k), t, ACT.Copy))
            else:
                h = self.act.sig(activation(hi(k), t, ACT.Identity, bias=shift(k)))
            return (t, h)

        def make(k):
            while len(begun) <= min(k + 1, NT - 1):
                begun.append(start(len(begun)))
            t, h = begun[k]
            self.dve.wait(h)
            if shift is None:
                u = self.dve.sig(tensor_tensor(lo(k), t, hi(k).bitcast(F32), ALU.subtract))
            else:
                u = self.dve.sig(scalar_tensor_tensor(
                    lo(k), t, shift(k), hi(k).bitcast(F32), ALU.add, ALU.subtract))
            b["tfree"][k % 3] = u
            return u
        return make


def halves(p, name, n, width, kb):
    hi = p.sb(name + "h", [128, n, width], F32R, kb)
    lo = p.sb(name + "l", [128, n, width], F32R, kb + n * width / 256)
    return hi, lo


def tile_of(t, a=None, b=None):
    if a is None:
        return lambda k: t[:, k, :]
    return lambda k: t[:, k, a:b]


def late_split(p, src, hi, lo, n, ready, ahead=2):
    def make(k):
        p.act.wait(*ready)
        p.dve.wait(*ready)
        h = p.act.sig(activation(hi(k), src(k), ACT.Copy))
        p.dve.wait(h, *ready)
        return p.dve.sig(tensor_tensor(lo(k), src(k), hi(k).bitcast(F32), ALU.subtract))
    return Operand(hi, lo, n, make, ahead=ahead)


def attention_a(p, q, k, v, sb):
    act, dve, pe, PS = p.act, p.dve, p.pe, p.PS
    Sx, PT, st = sb["S"], sb["PT"], sb["st"]
    for h in range(4):
        for qb in range(2):
            nk = 128 * (qb + 1)
            if 0 < 2 * h + qb < 6:
                yield
            elif h + qb == 0:
                yield
                yield
            pe.wait(*p.tk["qkv"], *p.bank_free[4], *p.bank_free[5])
            for g in range(3):
                o = PS[4 + g // 2][:, (g % 2) * 256:(g % 2) * 256 + nk]
                f = (matmul(o, q[:, 4 * g + h, qb * 128:qb * 128 + 128],
                                                  k[:, 4 * g + h, 0:nk], start=True, stop=True,
                                                  skip_group_check=True))
                t = pe.sig(f)
            yield
            dve.wait(t, p.tk.get("Sfree"), p.tk["cst"])
            for g in range(3):
                o = PS[4 + g // 2][:, (g % 2) * 256:(g % 2) * 256 + nk]
                slope = float(np.float32(2.0) ** np.float32(-8.0 * (4 * g + h + 1) / 12))
                t = dve.sig(scalar_tensor_tensor(
                    Sx[:, g, 0:nk], sb["bias"][:, g, qb, 0:nk], slope, o, ALU.mult, ALU.add))
            p.bank_free[4] = p.bank_free[5] = [t]
            dve.wait(t)
            t = dve.sig(tensor_reduce(st[:, 0:1], Sx[:, :, 0:nk], AX.XY, ALU.max))
            dve.wait(t)
            t = dve.sig(tensor_scalar(st[:, 1:2], st[:, 0:1], -1.0, None, ALU.mult))
            act.wait(t)
            t = act.sig(activation(Sx[:, :, 0:nk], Sx[:, :, 0:nk], ACT.Exp, bias=st[:, 1:2],
                                               accum_out=st[:, 2:3]))
            yield
            yield
            dve.wait(t)
            t = dve.sig(reciprocal(st[:, 3:4], st[:, 2:3]))
            dve.wait(t)
            t = dve.sig(tensor_scalar(Sx[:, :, 0:nk], Sx[:, :, 0:nk], st[:, 3:4], None, ALU.mult))
            yield
            pe.wait(t, *p.bank_free[4], *p.bank_free[5])
            blocks = [(g, kb) for g in range(3) for kb in range(qb + 1)]
            for i, (g, kb) in enumerate(blocks):
                o = PS[4 + i // 4][:, (i % 4) * 128:(i % 4) * 128 + 128]
                t = pe.sig(transpose(
                    o, Sx[:, g, kb * 128:kb * 128 + 128], p.cst[:, 0:128]))
            p.tk["Sfree"] = t
            act.wait(t, p.tk.get("PTfree"))
            n0 = min(len(blocks), 4) * 128
            t = act.sig(activation(PT[:, 0:n0], PS[4][:, 0:n0], ACT.Copy))
            p.bank_free[4] = [t]
            if len(blocks) > 4:
                n1 = len(blocks) * 128 - 512
                t = act.sig(activation(PT[:, 512:512 + n1], PS[5][:, 0:n1], ACT.Copy))
                p.bank_free[5] = [t]
            yield
            if 2 * h + qb < 6:
                yield
            pe.wait(t, *p.bank_free[6])
            for i, (g, kb) in enumerate(blocks):
                c0 = (4 * g + h) * 128
                t = pe.sig(matmul(
                    PS[6][:, 0:128], v[:, kb, c0:c0 + 128], PT[:, i * 128:i * 128 + 128],
                    start=(i == 0), stop=(i == len(blocks) - 1), skip_group_check=True))
            p.tk["PTfree"] = t
            act.wait(t)
            t = act.sig(activation(sb["ya"][:, h, qb * 128:qb * 128 + 128], PS[6][:, 0:128], ACT.Copy))
            p.bank_free[6] = [t]
            p.tk["ya"] = t
            yield


def attention_b(p, q, k, v, sb):
    act, dve, pe, PS = p.act, p.dve, p.pe, p.PS
    Z, E, R = sb["z"], sb["e"], sb["r"]
    ms = p.cst[:, CB["ms"]:CB["ms"] + 384]
    tri = p.cst[:, CB["tri"]:CB["tri"] + 128]
    B = PS[7]
    for h in range(4):
        for _ in range(2 + (h > 0)):
            yield
        pe.wait(*p.tk["qkv"], *p.bank_free[7])
        pe.run(matmul(B[:, 0:256], k[:, h, 0:128], q[:, h, :], start=True, stop=True,
                                  skip_group_check=True))
        t = pe.sig(matmul(B[:, 256:384], k[:, h, 128:256], q[:, h, 128:256], start=True, stop=True,
                                      skip_group_check=True))
        yield
        dve.wait(t, p.tk["cst"])
        z = dve.sig(tensor_copy(Z[:, :], B[:, 0:384]))
        act.wait(z)
        t = act.sig(activation(E[:, :], Z[:, :], ACT.Abs))
        act.wait(t)
        t = act.sig(activation(E[:, :], E[:, :], ACT.Exp, scale=-1.0))
        act.wait(t)
        l = act.sig(activation(E[:, :], E[:, :], ACT.Ln, bias=1.0))
        yield
        yield
        dve.wait(l, z)
        t = dve.sig(scalar_tensor_tensor(R[:, :], Z[:, :], 0.0, E[:, :], ALU.max, ALU.add))
        dve.wait(t)
        t2 = dve.sig(tensor_tensor(Z[:, :], Z[:, :], R[:, :], ALU.subtract))
        t = dve.sig(tensor_tensor(R[:, :], R[:, :], ms, ALU.mult))
        yield
        yield
        pe.wait(t)
        pe.run(matmul(B[:, 0:256], tri, R[:, 0:256], start=True, stop=True, skip_group_check=True))
        pe.run(matmul(B[:, 128:256], p.ones[:, :], R[:, 256:384], start=False, stop=True,
                                  skip_group_check=True))
        t = pe.sig(matmul(B[:, 256:384], tri, R[:, 256:384], start=False, stop=True,
                                      skip_group_check=True))
        yield
        dve.wait(t, t2)
        t = dve.sig(tensor_tensor(Z[:, :], Z[:, :], B[:, 0:384], ALU.subtract))
        act.wait(t)
        t = act.sig(activation(Z[:, :], Z[:, :], ACT.Exp))
        dve.wait(t)
        t = dve.sig(tensor_tensor(Z[:, :], Z[:, :], ms, ALU.mult))
        yield
        yield
        yield
        pe.wait(t)
        pe.run(matmul(B[:, 0:256], v[:, 0, h * 128:h * 128 + 128], Z[:, 0:256], start=True, stop=True,
                                  skip_group_check=True))
        t = pe.sig(matmul(B[:, 128:256], v[:, 1, h * 128:h * 128 + 128], Z[:, 256:384],
                                      start=False, stop=True, skip_group_check=True))
        yield
        act.wait(t)
        dve.wait(t)
        t = act.sig(activation(sb["yb"][:, h, :], B[:, 0:256], ACT.Copy))
        p.bank_free[7] = [t]
        p.tk["yb"] = t
        yield


def first_block(p):
    act, dve, pe, pool, PS, A, F = p.act, p.dve, p.pe, p.pool, p.PS, p.A, p.F
    H = p.H
    nb = p.norm_buffers("a", F + 80)
    Uh, Ul = halves(p, "U", NT, T, F)
    for i in range(8):
        p.sq_add(nb, H[:, 2 * i:2 * i + 2, :], [p.tk["x"][i // 2]], direct=True)
    dve.wait(p.tk["x"][3], p.tk["vec"])
    p.rstd(nb)
    U = Operand(tile_of(Uh), tile_of(Ul), NT,
                p.scaled(nb, tile_of(H), lambda k: p.v("g_mix_pre", k), None, tile_of(Uh), tile_of(Ul)), ahead=3)
    b = F + 32
    qa = p.sb("qa", [128, 12, T], F32, b)
    ka = p.sb("ka", [128, 12, T], F32, b + 12)
    va = p.sb("va", [128, 2, 1536], F32, b + 24)
    qb_ = p.sb("qb", [128, 4, T], F32, b + 36)
    kb_ = p.sb("kb", [128, 4, T], F32, b + 40)
    vb = p.sb("vb", [128, 2, 512], F32, b + 44)
    W = A["w_in"]
    toks = []

    def plain(dst, scale):
        def evac(s, t):
            act.wait(t)
            for i in range(2):
                u = act.sig(activation(dst(i), PS[2 * s + i][:, :], ACT.Copy, scale=scale))
            p.set_free[s] = [u]
            toks.append(u)
        return evac

    def fm(t, m):
        return lambda i: t[:, m + 2 * i:m + 2 * i + 2, :]

    for g in range(20 - 8):
        tm = g in (6, 7, 8, 11)
        s, t = p.group(W, g * 512, 512, U, T, tm=tm)
        if g == 0:
            bounds(p)
        if g < 3:
            plain(fm(qa, 4 * g), QS)(s, t)
        elif g < 6:
            plain(fm(ka, 4 * (g - 3)), 1.0)(s, t)
        elif g < 9:
            plain(lambda i, g=g: va[:, i, (g - 6) * 512:(g - 5) * 512], 1.0)(s, t)
        elif g == 9:
            plain(fm(qb_, 0), QS)(s, t)
        elif g == 10:
            plain(fm(kb_, 0), 1.0)(s, t)
        else:
            plain(lambda i: vb[:, i, :], 1.0)(s, t)
    p.tk["qkv"] = toks[-1:]
    b = F + 80
    gt = p.sb("gt", [128, 32, T], F32, b)
    bias = p.sb("bias", [128, 3, 2, 256], F32, b + 32)
    sbx = {"bias": bias, "ya": qa, "yb": qb_,
           "S": p.sb("Sx", [128, 3, 256], F32, b + 38), "PT": p.sb("PT", [128, 768], F32, b + 41),
           "z": p.sb("z", [128, 384], F32, b + 44), "e": p.sb("e", [128, 384], F32, b + 45.5),
           "r": p.sb("r", [128, 384], F32, b + 47), "st": p.SM}
    p.tk["cst"] = p.load(bias[:, :, :, :], A["bias"].rearrange("p (a b c) -> p a b c", a=3, b=2), "bias",
                         [toks[-1]])
    p.gens = [attention_a(p, qa, ka, va, sbx), attention_b(p, qb_, kb_, vb, sbx)]
    for g in range(8):
        s, t = p.group(W, 6144 + g * 512, 512, U, T)
        act.wait(t)
        for i in range(2):
            u = act.sig(activation(gt[:, 4 * g + 2 * i:4 * g + 2 * i + 2, :],
                                                    PS[2 * s + i][:, :], ACT.Copy))
        p.set_free[s] = [u]
    gate_done = t
    p.finish()
    for b in (6, 7):
        dve.wait(*p.bank_free[b])
        p.bank_free[b] = [dve.sig(memset(PS[b][:, :], 0.0))]
    p.tk["rst"] = p.load(p.cst[:, 128:640], A["cst"][:, 640:1152], "rst", [p.tk["ya"], p.tk["yb"], p.bank_free[7][0]])
    YAh, YAl = halves(p, "YA", 4, T, F)
    YBh, YBl = halves(p, "YB", 4, T, F + 8)
    act.wait(gate_done)
    dve.wait(gate_done)
    YA = late_split(p, tile_of(qa), tile_of(YAh), tile_of(YAl), 4, [p.tk["ya"]])
    YB = late_split(p, tile_of(qb_), tile_of(YBh), tile_of(YBl), 4, [p.tk["yb"]])
    YA.ahead = YB.ahead = 3
    YA.need(3)
    YB.need(3)
    MIX = halves(p, "MIX", NT, T, F + 32)
    t1 = p.sb("mt1", [128, 1024], F32, F + 120)
    t2 = p.sb("mt2", [128, 1024], F32, F + 124)
    mtoks = []
    act.wait(u)
    for i in range(8):
        u = act.sig(activation(gt[:, 4 * i:4 * i + 4, :], gt[:, 4 * i:4 * i + 4, :], ACT.Sigmoid))
    sig = u
    mixfree = None
    p.pool_split = 3
    for g in range(4):
        sa, ta = p.group(A["w_ba"], g * 512, 512, YA, T)
        sb_, tb = p.group(A["w_bb"], g * 512, 512, YB, T)
        dve.wait(ta, sig, mixfree)
        for i in range(2):
            u = dve.sig(tensor_tensor(t1[:, 512 * i:512 * i + 512], PS[2 * sa + i][:, :],
                                                       gt[:, 4 * g + 2 * i:4 * g + 2 * i + 2, :], ALU.mult))
        p.set_free[sa] = [u]
        dve.wait(tb)
        for i in range(2):
            u = dve.sig(tensor_tensor(t2[:, 512 * i:512 * i + 512], PS[2 * sb_ + i][:, :],
                                                       gt[:, 16 + 4 * g + 2 * i:18 + 4 * g + 2 * i, :], ALU.mult))
        p.set_free[sb_] = [u]
        pool.wait(u)
        u = pool.sig(tensor_tensor(t1[:, :], t1[:, :], t2[:, :], ALU.add))
        act.wait(u)
        h = act.sig(activation(MIX[0][:, 4 * g:4 * g + 4, :], t1[:, :], ACT.Copy))
        dve.wait(h, u)
        u = dve.sig(tensor_tensor(MIX[1][:, 4 * g:4 * g + 4, :], t1[:, :],
                                                   MIX[0][:, 4 * g:4 * g + 4, :].bitcast(F32), ALU.subtract))
        mixfree = u
        mtoks += [u] * 4
    p.pool_split = 0
    p.ada_rate = ADA1
    X = Operand(tile_of(MIX[0]), tile_of(MIX[1]), NT, toks=mtoks)
    Y = p.sb("Yw", [128, NT, T], F32, F + 64)
    nb = p.norm_buffers("b", F + 104)
    out_groups(p, A["w_out"], X, Y, nb, T, 512, [lambda k: p.v("g_mix_post", k)], after=[mtoks[-1]])
    run_beside(p, residual(p, Y, nb, H, 0, nb), 4)
    p.pool_split = 2
    Uh, Ul = halves(p, "V", NT, T, F)
    U = Operand(tile_of(Uh), tile_of(Ul), NT,
                p.scaled(nb, tile_of(H), lambda k: p.v("g_ffn_pre", k), None, tile_of(Uh), tile_of(Ul)), ahead=3)
    AC = halves(p, "AC", NF, T, F + 32)
    cg = p.sb("cg", [128, 4, T], F32, F + 120)
    cv = p.sb("cv", [128, 4, T], F32, F + 124)
    atoks = []
    prod = None
    tails = []

    def product(g):
        u = dve.sig(tensor_tensor(cv[:, :, :], cg[:, :, :], cv[:, :, :], ALU.mult))
        act.wait(u)
        h = act.sig(activation(AC[0][:, 4 * g:4 * g + 4, :], cv[:, :, :], ACT.Copy))
        yield
        dve.wait(h, u)
        u = dve.sig(tensor_tensor(AC[1][:, 4 * g:4 * g + 4, :], cv[:, :, :],
                                  AC[0][:, 4 * g:4 * g + 4, :].bitcast(F32), ALU.subtract))
        tails.append(u)
        atoks.extend([u] * 4)
        yield

    for g in range(11):
        for half, buf in ((0, cg), (1, cv)):
            s, t = p.group(A["w_up"], half * DFF + g * 512, 512, U, T)
            p.pool_split = 0
            act.wait(t, tails[-1] if tails else None)
            for i in range(4):
                m = half * NF + 4 * g + i
                o = PS[2 * s + i // 2][:, (i % 2) * 256:(i % 2) * 256 + 256]
                u = act.sig(activation(
                    buf[:, i, :], o, ACT.Identity, scale=p.v("cw", 176 + m), bias=p.v("cb", m)))
            dve.wait(u)
            for n in (1, 2):
                for i in range(4):
                    m = half * NF + 4 * g + i
                    o = PS[2 * s + i // 2][:, (i % 2) * 256:(i % 2) * 256 + 256 - n]
                    w = dve.sig(scalar_tensor_tensor(
                        buf[:, i, n:], o, p.v("cw", (2 - n) * 88 + m), buf[:, i, n:], ALU.mult, ALU.add))
                if n == 1:
                    dve.wait(w)
            p.set_free[s] = [w]
            if half == 0:
                act.wait(w)
                gel = act.sig(activation(cg[:, :, :], cg[:, :, :], ACT.Gelu_apprx_tanh))
        dve.wait(gel, w)
        p.gens.append(product(g))
    p.finish()
    prod = tails[-1]
    X = Operand(tile_of(AC[0]), tile_of(AC[1]), NF, toks=atoks)
    Y = p.sb("Yd", [128, NT, T], F32, F)
    nb = p.norm_buffers("c", F + 16)
    down = out_groups(p, A["w_down"], X, Y, nb, T, 512, [lambda k: p.v("g_ffn_post", k)], after=[prod])
    PF = p.sb("PF", [128, 2, T], F32, F + 120)
    E = p.sb("E", [128, NT, T], F32, F + 96)
    ptok = p.load(PF[:, :, :], A["pT"].rearrange("(k p) t -> p k t", p=128), "pf", [prod])
    XP = Operand(tile_of(PF), None, 2, toks=[ptok] * 2)
    HC = halves(p, "HC", NT, 2 * T, F + 32)
    hh, hl = tile_of(HC[0], 0, T), tile_of(HC[1], 0, T)
    due = [down]
    XG = late_split(p, tile_of(H), hh, hl, NT, due, ahead=0)

    def split_up(k, n, h):
        due.append(h)
        XG.need(k + n - 1)

    rest = residual(p, Y, nb, H, 0, then=split_up)
    for n in range(4):
        next(rest)
        p.ada((0, 2, 2, 0)[n])
    for g in range(4):
        s, t = p.group(A["w_ple_in"], g * 512, 512, XP, T, raw=True, quiet=True)
        act.wait(t, down)
        for i in range(2):
            u = act.sig(activation(E[:, 4 * g + 2 * i:4 * g + 2 * i + 2, :], PS[2 * s + i][:, :], ACT.Copy))
        p.set_free[s] = [u]
    etok = u
    p.gens = [rest]
    p.finish()
    X = XG
    CX = p.sb("CX", [128, NT, T], F32, F + 112)
    tmp = p.sb("ptmp", [128, 1024], F32, F)
    while p.ada_at < 96:
        p.ada(1)
    p.mods(0)
    nc_ = p.norm_buffers("e", F + 4, bank=4)
    nl = p.norm_buffers("d", F + 16)
    p.gens = [context(p, nc_, CX, HC, [down, etok, t])]
    p.pool_split = 2
    last = None

    def squares(g, after):
        if g < 3:
            yield
            yield
        for i in (4 * g, 4 * g + 2):
            p.sq_add(nl, H[:, i:i + 2, :], [after], direct=(g == 3))
        yield

    for g in range(4):
        s, t = p.group(A["w_ple_gate"], g * 512, 512, X, T)
        act.wait(t, last)
        for i in range(2):
            u = act.sig(activation(tmp[:, 512 * i:512 * i + 512], PS[2 * s + i][:, :], ACT.Sigmoid))
        p.set_free[s] = [u]
        lane = dve if g == 3 else pool
        lane.wait(u, etok, last)
        u = lane.sig(tensor_tensor(tmp[:, :], tmp[:, :], E[:, 4 * g:4 * g + 4, :], ALU.mult))
        lane.wait(u)
        last = lane.sig(tensor_tensor(H[:, 4 * g:4 * g + 4, :], H[:, 4 * g:4 * g + 4, :], tmp[:, :], ALU.add))
        p.gens.append(squares(g, last))
        if g == 3:
            p.finish()
    p.pool_split = 0
    p.finish()
    p.tk["H"] = last
    p.tk["hpe"] = t
    return HC, nl


def context(p, nb, CX, HC, after):
    yield
    p.tk["cx"] = p.load(CX[:, :, :], p.A["ctxT"].rearrange("(k p) t -> p k t", p=128), "cx", after + [(p.s_mm, len(p.chunks) - 1)])
    for _ in range(4):
        yield
    for i in range(8):
        p.sq_add(nb, CX[:, 2 * i:2 * i + 2, :], [p.tk["cx"], p.tk["G"]])
        yield
    p.dve.wait(p.tk["cx"])
    yield from p.rstd_steps(nb)
    p.tk["ctx"] = p.scaled(nb, tile_of(CX), lambda k: p.coef(0, 0, 1, k), lambda k: p.shift(0, 1, k),
                           tile_of(HC[0], T, 2 * T), tile_of(HC[1], T, 2 * T))
    for k in range(NT):
        p.tk["ctx"](k)
        yield


def out_groups(p, W, X, Y, nb, N, cols, coefs, after=(), lag=False):
    per = cols // 128
    n = X.n * cols // 1024
    begun = [p.group(W, g * cols, cols, X, N, part=(0, n - 1))[0] for g in range(2)] if lag else []
    for g in range(D // cols):
        if g < len(begun):
            s, t = p.group(W, g * cols, cols, X, N, part=(n - 1, n), s=begun[g])
        else:
            s, t = p.group(W, g * cols, cols, X, N)
        p.act.wait(t, *after)
        for i in range(2):
            k = g * per + i * (512 // N)
            ps = p.PS[2 * s + i][:, :]
            u = p.sq_add(nb, ps, direct=(g == D // cols - 1))
            for m in range(2):
                kk, c0 = (k + m, 0) if N == T else (k, T * m)
                u = p.act.sig(activation(Y[:, kk, c0:c0 + T], p.PS[2 * s + i][:, T * m:T * m + T], ACT.Copy,
                                         scale=coefs[0 if N == T else m](kk)))
        p.set_free[s] = [u]
    p.tk["Y"] = u
    return t


def residual(p, Y, nb, H, c0, again=None, out=None, then=None):
    yield
    if c0 == 0:
        yield from p.rstd_steps(nb)
        yield
    due = []

    def part(lane, k, n):
        rs = nb["rs"][:, c0:c0 + T].unsqueeze(1).to_broadcast([128, n, T])
        y = Y[:, k:k + n, c0:c0 + T]
        u = lane.sig(tensor_tensor(y, y, rs, ALU.mult))
        lane.wait(u)
        return lane.sig(tensor_tensor(H[:, k:k + n, :], H[:, k:k + n, :], y, ALU.add))

    def square(k, n, h):
        if again is not None:
            p.act.wait(h)
            t = p.act.sig(activation(Y[:, k:k + n, c0:c0 + T], H[:, k:k + n, :], ACT.Square))
            due.append((k, n, t))
        if out is not None:
            p.load(out[:, k:k + n, :], H[:, k:k + n, :], "out", [h], lane=p.last)
        if then is not None:
            then(k, n, h)

    def add():
        while due:
            k, n, t = due.pop(0)
            for i in range(k, k + n):
                p.pe.wait(t)
                if not again["begun"]:
                    p.pe.wait(*p.bank_free[again["bank"]])
                p.pe.sig(matmul(p.PS[again["bank"]][0:1, 0:T], p.ones[:, 0:1], Y[:, i, c0:c0 + T],
                                start=not again["begun"], stop=True, skip_group_check=True))
                again["begun"] = True

    p.dve.wait(p.tk["Y"])
    p.pool.wait(p.tk["Y"], nb["rst"], p.tk["H"])
    a = part(p.pool, 11, 3)
    b = part(p.pool, 14, 2)
    square(0, 4, part(p.dve, 0, 4))
    yield
    square(4, 4, part(p.dve, 4, 4))
    yield
    square(8, 3, part(p.dve, 8, 3))
    square(11, 3, a)
    yield
    p.dve.wait(a, b)
    square(14, 2, b)
    h = p.dve.sig(tensor_copy(p.SM[:, 26:27], p.ones[:, 0:1]))
    yield
    p.tk["H"] = h
    if again is not None:
        add()
        yield from p.rstd_steps(again)
    yield


def run_beside(p, gen, n):
    if gen is not None:
        p.gens.append(gen)
    for _ in range(n):
        p.pump()
        p.ada(1)
    p.finish()


def second_block(p, HC, nb):
    act, dve = p.act, p.dve
    H = p.H
    Hh, Hl = HC
    p.rstd(nb)
    act.wait(p.tk["hpe"], p.tk["G"])
    dve.wait(p.tk["hpe"], p.tk["G"])
    X = Operand(tile_of(Hh), tile_of(Hl), NT,
                p.scaled(nb, tile_of(H), lambda k: p.coef(0, 0, 0, k), lambda k: p.shift(0, 0, k),
                         tile_of(Hh, 0, T), tile_of(Hl, 0, T)), ahead=2)
    layer0(p, X, HC)


def layer0(p, X, HC):
    act, dve, pe, PS, A, F = p.act, p.dve, p.pe, p.PS, p.A, p.F
    H = p.H
    N = 2 * T
    W = A["ev_w_in"]
    CC = p.sb("CC", [128, NT, N], F32, F + 96)
    AV = p.sb("AV", [128, 4, 256], F32, F)
    PL = p.sb("PL", [128, 2, N], F32, F + 4)
    MX = p.sb("MX", [128, 2, N], F32, F + 8)
    MM = p.sb("MM", [128, 4, 256], F32, F + 12)
    T1 = p.sb("T1", [128, 2, N], F32, F + 16)
    T2 = p.sb("T2", [128, 2, N], F32, F + 20)
    T3 = p.sb("T3", [128, 2, N], F32, F + 24)
    free = {"AV": None, "PL": None, "MX": None, "MM": None, "T1": None, "T2": None, "T3": None}
    p.ada_rate = ADA2

    def pooling(j, av, mm):
        yield
        for ct in range(2):
            pe.wait(av, mm, *p.bank_free[4 + ct])
            for w in range(2):
                for tk in range(2):
                    o = PS[4 + ct][:, w * 256:w * 256 + 256]
                    t = pe.sig(matmul(
                        o, AV[:, 2 * w + tk, ct * 128:ct * 128 + 128], MM[:, 2 * w + tk, :],
                        start=(w == 0 and tk == 0), stop=(tk == 1), skip_group_check=True))
        free["AV"] = free["MM"] = t
        yield
        for ct in range(2):
            act.wait(t, free["PL"])
            u = act.sig(activation(PL[:, ct, :], PS[4 + ct][:, :], ACT.Copy))
            p.bank_free[4 + ct] = [u]
        free["PLw"] = u
        yield

    def banks(s):
        return [PS[2 * s][:, :], PS[2 * s + 1][:, :]]

    xdone = None
    for j in range(4):
        if j == 0:
            s, t = p.group(W, 256 * j, 256, X, N, tm=True)
            xdone = t
            mm = p.load(MM[:, :, :], A["poolm"][j].rearrange("p (a b) -> p a b", a=4), "mm", [t])
        else:
            mm = p.load(MM[:, :, :], A["poolm"][j].rearrange("p (a b) -> p a b", a=4), "mm", [free["MM"]])
            s, t = p.group(W, 256 * j, 256, X, N, tm=True)
        act.wait(t, free["AV"])
        for i in range(2):
            u = act.sig(activation(AV[:, 2 * i:2 * i + 2, :], banks(s)[i], ACT.Copy))
        p.set_free[s] = [u]
        g = pooling(j, u, mm)
        p.gens.append(g)
        s, t = p.group(W, 2048 + 256 * j, 256, X, N)
        act.wait(t, free["T1"])
        for i in range(2):
            u = act.sig(activation(T1[:, i, :], banks(s)[i], ACT.Copy))
        p.set_free[s] = [u]
        bx = u
        p.finish(g)
        XP = Operand(tile_of(PL), None, 2, toks=[free["PLw"]] * 2)
        s, t = p.group(A["ev_pool_w"][j], 0, 256, XP, N, raw=True)
        free["PL"] = t
        dve.wait(t, free["MX"])
        for i in range(2):
            u = dve.sig(tensor_scalar(MX[:, i, :], banks(s)[i], p.v("pscale", 2 * j + i),
                                                            None, ALU.mult))
        p.set_free[s] = [u]
        mxw = u
        s, t = p.group(W, 4096 + 256 * j, 256, X, N)
        dve.wait(t, bx, free["T2"])
        for i in range(2):
            u = dve.sig(tensor_tensor(T2[:, i, :], banks(s)[i], T1[:, i, :], ALU.mult))
        p.set_free[s] = [u]
        act.wait(u, free["T3"])
        free["T1"] = u
        for i in range(2):
            m = 2 * j + i
            c = act.sig(activation(T3[:, i, :], T2[:, i, :], ACT.Identity,
                                                         scale=p.v("ecw", 8 + m), bias=p.v("ecb", m)))
        dve.wait(c, u)
        for n in range(2):
            for i in range(2):
                m = 2 * j + i
                a = T2[:, i, :].rearrange("p (w t) -> p w t", w=2)
                y = T3[:, i, :].rearrange("p (w t) -> p w t", w=2)
                if n == 0:
                    a, y, w = a[:, :, 0:T - 1], y[:, :, 1:T], p.v("ecw", m)
                else:
                    a, y, w = a[:, :, 1:T], y[:, :, 0:T - 1], p.v("ecw", 16 + m)
                u = dve.sig(scalar_tensor_tensor(y, a, w, y, ALU.mult, ALU.add))
            dve.wait(u)
        free["T2"] = u
        s, t = p.group(W, 3072 + 256 * j, 256, X, N)
        dve.wait(t, u)
        for i in range(2):
            u = dve.sig(tensor_tensor(T3[:, i, :], banks(s)[i], T3[:, i, :], ALU.mult))
        p.set_free[s] = [u]
        bb = u
        for c0, dst, src in ((5120, 8 + 2 * j, T3), (1024, 2 * j, MX)):
            s, t = p.group(W, c0 + 256 * j, 256, X, N)
            if j == 3 and c0 == 1024:
                due = [t, free["T1"]]
                XO = late_split(p, tile_of(CC), tile_of(p.HC[0]), tile_of(p.HC[1]), NT, due)
                XO.ahead = 0
                XO.need(1)
            act.wait(t, free["T1"])
            for i in range(2):
                u = act.sig(activation(T1[:, i, :], banks(s)[i], ACT.Sigmoid))
            dve.wait(u, bb, mxw)
            for i in range(2):
                u = dve.sig(tensor_tensor(T1[:, i, :], banks(s)[i], T1[:, i, :], ALU.mult))
            p.set_free[s] = [u]
            dve.wait(u)
            if j == 0:
                dve.wait(xdone)
            u = dve.sig(tensor_tensor(CC[:, dst:dst + 2, :], T1[:, :, :],
                                                                    src[:, :, :], ALU.mult))
            free["T1"] = u
            free["T3" if src is T3 else "MX"] = u
    inproj = t
    p.finish()
    act.wait(inproj)
    dve.wait(inproj)
    due.append(u)
    X = XO
    X.ahead = 3
    Y = p.sb("Y0", [128, NT, N], F32, F + 96)
    CX = p.sb("CX2", [128, NT, T], F32, F)
    p.tk["cx"] = p.load(CX[:, :, :], A["ctxT"].rearrange("(k p) t -> p k t", p=128), "cx", [inproj, u])
    nb = p.norm_buffers("f", F + 16, N=512, acc=False)
    nb["acc"] = p.sb("accf", [128, 512], F32, F + 20)
    out_groups(p, A["ev_w_out"], X, Y, nb, N, 256,
               [lambda k: p.coef(0, 1, 0, k), lambda k: p.coef(0, 1, 1, k)])
    wout = (p.s_mm, len(p.chunks))
    while p.ada_at < 192 - 4:
        p.ada(1)
    p.dve.wait(p.tk["cx"])
    nl = p.norm_buffers("g", F + 16, bank=4, rs=F + 23, share=nb, acc=False)
    nc_ = p.norm_buffers("h", F + 16, bank=4, rs=F + 24, share=nb, acc=False)
    run_beside(p, residual(p, Y, nb, H, 0, nl), 4)
    p.mods(1)
    layer1(p, nl, nc_, CX, wout, residual(p, Y, nb, CX, T, nc_))


def layer1(p, nl, nc_, CX, wout, rest):
    act, dve, pe, PS, A, F = p.act, p.dve, p.pe, p.PS, p.A, p.F
    H = p.H
    N = 2 * T
    XH, XL = p.HC
    act.wait(wout, p.tk["G"])
    dve.wait(wout, p.tk["G"])
    mx = p.scaled(nl, tile_of(H), lambda k: p.coef(1, 0, 0, k), lambda k: p.shift(1, 0, k),
                  tile_of(XH, 0, T), tile_of(XL, 0, T))
    mc = p.scaled(nc_, tile_of(CX), lambda k: p.coef(1, 0, 1, k), lambda k: p.shift(1, 1, k),
                  tile_of(XH, T, N), tile_of(XL, T, N))
    XQ = Operand(tile_of(XH, 0, T), tile_of(XL, 0, T), NT, mx, ahead=2)
    X = Operand(tile_of(XH), tile_of(XL), NT, mc, ahead=2)
    W = A["od_w_in"]
    V = p.sb("hV", [128, 4, 256], F32, F)
    Q = p.sb("hQ", [128, 2, T], F32, F + 28)
    G = p.sb("hG", [128, 2, T], F32, F + 30)
    Aa = p.sb("hA", [128, 2, N], F32, F + 4)
    B = p.sb("hB", [128, 2, N], F32, F + 8)
    C = p.sb("hC", [128, 2, N], F32, F + 12)
    KI = p.sb("hKI", [128, 2, T], F32, F + 16)
    QD = p.sb("hQD", [128, 2, T], F32, F + 18)
    ST = p.sb("hST", [128, 2, 4, 128], F32, F + 20)
    SC = p.sb("hSC", [128, 2, 2, 128], F32, F + 24)
    OT = p.sb("hOT", [128, 4, 128], F32, F + 26)
    OH, OL = halves(p, "O", NT, T, F + 96)
    rst = p.cst[:, CB["rst"]:CB["rst"] + 512]
    KD = B[:, :, :].rearrange("p h (a b) -> p h a b", a=4)
    f = {n: None for n in ("V", "Q", "G", "A", "B", "C", "KI", "QD", "ST", "SC", "OT", "O", "DEC", "OTr")}
    dec = p.DEC

    def direction(j, d, ztok, vtok, qtok):
        last = 63 if d == 0 else 0
        B16 = B[:, :, :].rearrange("p h (n c) -> p (h n) c", c=64)
        A16 = Aa[:, :, :].rearrange("p h (n c) -> p (h n) c", c=64)
        act.wait(ztok)
        lns = [None, None]
        for h in range(2):
            k = 2 * j + h
            t = act.sig(activation(
                Aa[:, h, :], Aa[:, h, :], ACT.Ln, scale=p.LB[:, 32 + 16 * d + k:33 + 16 * d + k],
                bias=p.LB[:, 16 * d + k:16 * d + k + 1]))
            lns[h] = t
        yield
        dve.wait(f["B"], p.tk["rst"])
        for h in range(2):
            dve.wait(lns[h])
            if d == 0:
                t = dve.sig(tensor_tensor_scan(B[:, h, :], rst, Aa[:, h, :], 0.0,
                                                                ALU.mult, ALU.add))
            else:
                t = dve.sig(tensor_tensor_scan(B[:, h, ::-1], rst, Aa[:, h, ::-1], 0.0,
                                                                ALU.mult, ALU.add))
        dve.wait(t)
        dl = dve.sig(tensor_tensor(A16, B16[:, :, last:last + 1].to_broadcast([128, 16, 64]), B16, ALU.subtract))
        yield
        act.wait(t, f["KI"], f["QD"], f["DEC"])
        act.run(activation(dec[:, 0:16], B16[:, :, last], ACT.Exp))
        act.run(activation(KI[:, :, :], B[:, :, 0:T], ACT.Exp, scale=-1.0))
        act.run(activation(QD[:, :, :], B[:, :, 0:T], ACT.Exp))
        act.wait(dl)
        a = act.sig(activation(Aa[:, :, :], Aa[:, :, :], ACT.Exp))
        yield
        dve.wait(a, qtok)
        oms = [p.LB[:, 32 + 16 * d + 2 * j + h:33 + 16 * d + 2 * j + h] for h in range(2)]
        for h in range(2):
            u = dve.sig(scalar_tensor_tensor(Aa[:, h, :], C[:, h, :], oms[h], Aa[:, h, :], ALU.mult, ALU.mult))
        qd = f["Q"] = dve.sig(tensor_tensor(QD[:, :, :], Q[:, :, :], QD[:, :, :], ALU.mult))
        yield
        for h in range(2):
            ki = f["C"] = dve.sig(scalar_tensor_tensor(KI[:, h, :], C[:, h, 0:T], oms[h], KI[:, h, :],
                                                       ALU.mult, ALU.mult))
        yield
        yield
        order = [4, 5, 6, 7, 0, 1, 2, 3] if d == 0 else [7, 6, 5, 4, 3, 2, 1, 0]

        def turn(h):
            pe.wait(u, *p.bank_free[4])
            for i in range(4):
                t = pe.sig(transpose(PS[4][:, i * 128:i * 128 + 128], Aa[:, h, i * 128:i * 128 + 128],
                                     p.cst[:, 0:128]))
            f["A"] = t
            act.wait(t)
            kd = act.sig(activation(B[:, h, :], PS[4][:, :], ACT.Copy))
            p.bank_free[4] = [kd]
            return kd

        def ds(n):
            return PS[5 + n % 2][:, 128 * (n // 2):128 * (n // 2) + 128]

        def states(h, kd):
            pe.wait(kd, vtok, qd, ki, *p.bank_free[5], *p.bank_free[6])
            for n in order[:7]:
                r = 64 * (n % 2)
                pe.run(matmul(ds(n), KD[r:r + 64, h, n // 2, :], V[r:r + 64, n // 2, h * 128:h * 128 + 128],
                              start=True, stop=True, skip_group_check=True))
            for i in range(2):
                c = 128 * i
                t = pe.sig(matmul(PS[4][:, c:c + 128], KI[:, h, c:c + 128], QD[:, h, c:c + 128],
                                  start=True, stop=True, skip_group_check=True))
            f["B"] = f["KI"] = t
            dve.wait(t, f["SC"], f["ST"])
            sc = dve.sig(tensor_tensor(
                SC[:, h, :, :].bitcast(I32), PS[4][:, 0:256].bitcast(I32).rearrange("p (a b) -> p a b", a=2),
                p.hgm[:, 128 * d:128 * d + 128].unsqueeze(1).to_broadcast([128, 2, 128]), ALU.bitwise_and))
            p.bank_free[4] = [sc]
            s0 = order[4]
            u = dve.sig(tensor_copy(ST[:, h, s0, :], ds(order[0])))
            for i in range(1, 7):
                n = order[i]
                frm, to = (s0, s0) if i < 4 else (n, order[i + 1])
                dve.wait(u)
                u = dve.sig(scalar_tensor_tensor(
                    ST[:, h, to, :], ST[:, h, frm, :], dec[:, 8 * h + n:8 * h + n + 1], ds(n), ALU.mult, ALU.add))
            p.bank_free[5] = p.bank_free[6] = [u]
            f["DEC"] = u
            return u

        def outputs(h, st):
            pe.wait(st)
            if d == 0 and h == 0:
                pe.wait(*p.bank_free[7])
            for n in range(4):
                r, c = 64 * (n % 2), 256 * h + 128 * (n // 2)
                pe.run(matmul(PS[7][r:r + 64, c:c + 128], QD[:, h, n * 64:n * 64 + 64], ST[:, h, n, :],
                              start=(d == 0 and h == 0 and n < 2), stop=False, skip_group_check=True))
            for i in range(2):
                c = 256 * h + 128 * i
                t = pe.sig(matmul(PS[7][:, c:c + 128], SC[:, h, i, :], V[:, i, h * 128:h * 128 + 128],
                                  start=False, stop=(d == 1), skip_group_check=True))
            f["QD"] = f["ST"] = f["SC"] = f["V"] = f["O"] = t

        kd = turn(0)
        yield
        st0 = states(0, kd)
        yield
        kd = turn(1)
        yield
        outputs(0, st0)
        st1 = states(1, kd)
        yield
        yield
        outputs(1, st1)
        yield

    def readout(j, gtok):
        act.wait(f["O"], f["OTr"])
        for i in range(4):
            t = act.sig(activation(OT[:, i, :], PS[7][:, 128 * i:128 * i + 128], ACT.Square,
                                   accum_out=p.SM[:, i:i + 1]))
        dve.wait(t)
        t = dve.sig(tensor_scalar(p.SM[:, 4:8], p.SM[:, 0:4], 1.0 / 128, EPS, ALU.mult, ALU.add))
        act.wait(t)
        t = act.sig(activation(p.SM[:, 4:8], p.SM[:, 4:8], ACT.Sqrt))
        dve.wait(t)
        t = dve.sig(reciprocal(p.SM[:, 4:8], p.SM[:, 4:8]))
        yield
        yield
        act.wait(t)
        for i in range(4):
            t = act.sig(activation(OT[:, i, :], PS[7][:, 128 * i:128 * i + 128], ACT.Copy,
                                   scale=p.SM[:, 4 + i:5 + i]))
        p.bank_free[7] = [t]
        yield
        pe.wait(t, *p.bank_free[4])
        for i in range(4):
            t = pe.sig(transpose(PS[4][:, 128 * i:128 * i + 128], OT[:, i, :], p.cst[:, 0:128]))
        dve.wait(t, gtok)
        for h in range(2):
            t = dve.sig(scalar_tensor_tensor(G[:, h, :], PS[4][:, 256 * h:256 * h + 256], p.v("onorm", 2 * j + h),
                                             G[:, h, :], ALU.mult, ALU.mult))
        p.bank_free[4] = [t]
        f["OTr"] = t
        act.wait(t)
        h_ = act.sig(activation(OH[:, 2 * j:2 * j + 2, :], G[:, :, :], ACT.Copy))
        dve.wait(h_, t)
        t = dve.sig(tensor_tensor(OL[:, 2 * j:2 * j + 2, :], G[:, :, :],
                                  OH[:, 2 * j:2 * j + 2, :].bitcast(F32), ALU.subtract))
        f["G"] = t
        otoks.extend([t, t])
        yield

    otoks = []
    p.serial = True

    def values(j):
        s, t = p.group(W, 4096 + 256 * j, 256, X, N, tm=True)
        p.finish(*works)
        act.wait(t, f["V"])
        for i in range(2):
            u = act.sig(activation(V[:, 2 * i:2 * i + 2, :], PS[2 * s + i][:, :], ACT.Copy))
        p.set_free[s] = [u]
        return u, t

    def queries(j):
        s, t = p.group(W, 6144 + 256 * j, 256, XQ, T)
        act.wait(t, f["Q"])
        u = act.sig(activation(Q[:, :, :], PS[2 * s][:, :], ACT.Copy))
        p.set_free[s] = [u]
        return u

    def forget(j, d):
        s, t = p.group(W, 2048 * d + 256 * j, 256, X, N)
        p.finish(*works)
        act.wait(t, f["A"], f["C"])
        for i in range(2):
            act.run(activation(C[:, i, :], PS[2 * s + i][:, :], ACT.Sigmoid, scale=-1.0))
            u = act.sig(activation(Aa[:, i, :], PS[2 * s + i][:, :], ACT.Sigmoid))
        p.set_free[s] = [u]
        return u, t

    works = []
    def gates(j):
        s, t = p.group(W, 8192 + 256 * j, 256, XQ, T)
        act.wait(t, f["G"])
        u = act.sig(activation(G[:, :, :], PS[2 * s][:, :], ACT.Sigmoid))
        dve.wait(u)
        u = dve.sig(tensor_tensor(G[:, :, :], PS[2 * s][:, :], G[:, :, :], ALU.mult))
        p.set_free[s] = [u]
        return u

    for j in range(8):
        p.pool_split = 1 if j == 0 else 0
        qt = queries(j)
        if j == 0:
            p.gens = [rest]
            gt = gates(j)
            p.finish()
        vt = values(j)[0]
        zt = forget(j, 0)[0]
        if j > 0:
            p.finish(*reads)
        works = [direction(j, 0, zt, vt, qt)]
        p.gens += works
        if j > 0:
            gt = gates(j)
        zt, t = forget(j, 1)
        works = [direction(j, 1, zt, vt, qt)]
        reads = [readout(j, gt)]
        p.gens += works + reads
    inproj = t

    def late(k):
        p.finish()
        return otoks[k]

    X = Operand(tile_of(OH), tile_of(OL), NT, late, toks=otoks[:NT - 2])
    Y = p.sb("Y1", [128, NT, T], F32, F + 32)
    nb = p.norm_buffers("i", F + 48)
    act.wait(inproj)
    dve.wait(inproj)
    out_groups(p, A["od_w_out"], X, Y, nb, T, 512, [lambda k: p.coef(1, 1, 0, k)], lag=True)
    p.gens = [residual(p, Y, nb, H, 0,
                       out=A["out"].rearrange("(k p) t -> p k t", p=128))]
    p.finish()


ADA1 = 0.3
ADA2 = 0.75


def bounds(p):
    act, dve = p.act, p.dve
    for lane in (act, dve, p.pe):
        lane.wait(p.tk["vec"], p.tk["c0"], p.tk["hgm"])
    cv = p.v("c", 0, 32)
    t = act.sig(activation(p.S[:, :], cv, ACT.Sigmoid))
    dve.wait(t)
    p.tk["S"] = dve.sig(tensor_tensor(p.S[:, :], p.S[:, :], cv, ALU.mult))
    L = [p.vec[:, VEC["lb"]:VEC["lb"] + 96].rearrange("p (d i k) -> p d i k", d=2, i=3)[:, :, i, :] for i in range(3)]
    m = p.SM[:, 32:64].rearrange("p (d k) -> p d k", d=2)
    lb = p.LB[:, 0:32].rearrange("p (d k) -> p d k", d=2)
    om = p.LB[:, 32:64].rearrange("p (d k) -> p d k", d=2)
    t = dve.sig(tensor_tensor(m, L[0], L[1], ALU.max))
    dve.wait(t)
    t = dve.sig(tensor_tensor(m, m, L[2], ALU.max))
    dve.wait(t)
    for i in range(3):
        t = dve.sig(tensor_tensor(L[i], L[i], m, ALU.subtract))
    act.wait(t)
    for i in range(3):
        t = act.sig(activation(L[i], L[i], ACT.Exp))
    dve.wait(t)
    t = dve.sig(tensor_tensor(lb, L[0], L[1], ALU.add))
    dve.wait(t)
    t = dve.sig(tensor_tensor(m, lb, L[2], ALU.add))
    dve.wait(t)
    t = dve.sig(reciprocal(m, m))
    dve.wait(t)
    t = dve.sig(tensor_tensor(lb, lb, m, ALU.mult))
    dve.wait(t)
    p.tk["lb"] = dve.sig(tensor_scalar(om, lb, -1.0, 1.0, ALU.mult, ALU.add))
    act.wait(p.tk["lb"])


def build(nc, A):
    p = Program(nc, A)
    p.tk = {}
    act, dve, pe, pool = p.act, p.dve, p.pe, p.pool
    xT = A["xT"].rearrange("(k p) t -> p k t", p=128)
    p.tk["x"] = [p.load(p.H[:, 4 * i:4 * i + 4, :], xT[:, 4 * i:4 * i + 4, :], f"x{i}", lane=p.sp) for i in range(4)]
    p.tk["vec"] = p.load(p.vec[:, :], A["vec"], "vec")
    p.tk["c0"] = p.load(p.cst[:, :], A["cst"][:, 0:NCB], "cst")
    p.tk["hgm"] = p.load(p.hgm[:, :], A["hgm"], "hgm")
    dve.run(memset(p.ones[:, :], 1.0))
    p.tk["ones"] = dve.sig(memset(p.SM[:, 25:26], EPS))
    for lane in (act, pe):
        lane.wait(p.tk["ones"])
    dve.wait(p.tk["vec"], p.tk["c0"], p.tk["ones"])
    p.tk["H"] = p.tk["x"][3]
    HC, nb = first_block(p)
    p.HC = HC
    second_block(p, HC, nb)
    p.play_stream()
    p.sp.items += p.last.items
    p.sp.wait((p.s_ld["out"][0], p.s_ld["out"][1]))
    with nc.Block() as block:
        @block.sync
        def _(e):
            p.sp.play(e)

        @block.scalar
        def _(e):
            act.play(e)

        @block.vector
        def _(e):
            dve.play(e)

        @block.tensor
        def _(e):
            pe.play(e)

        @block.gpsimd
        def _(e):
            pool.play(e)


def constants():
    f = np.float32
    q = np.arange(T)[:, None]
    k = np.arange(T)[None, :]
    bias = np.full((3, 2, 128, 256), -1e38, f)
    for g, (win, dil) in enumerate(((128, 1), (512, 4), (2048, 16))):
        ok = (k <= q) & ((q - k) % dil == 0) & ((q - k) // dil <= win // dil)
        bias[g] = np.where(ok, -(q - k), -1e38).astype(f).reshape(2, 128, 256)
    bias = np.ascontiguousarray(bias.transpose(2, 0, 1, 3).reshape(128, -1))
    i = np.arange(128)
    cst = np.zeros((128, 1152), f)
    cst[:, 0:128] = np.eye(128)
    cst[:, 128:256] = i[:, None] > i[None, :]
    strict = i[:, None] < i[None, :]
    cst[:, 256:384] = strict
    cst[:, 384:512] = 1
    cst[:, 512:640] = strict
    cst[:, 640:1152] = (np.arange(512) % 64 != 0)[None]
    s, c = np.arange(128)[:, None], np.arange(128)[None, :]
    near = s // 64 == c // 64
    hgm = np.concatenate([near & (s <= c), near & (s >= c)], axis=1)
    hgm = np.where(hgm, -1, 0).astype(np.int32)

    def mean(n, w):
        t = np.arange(n)
        lo, hi = np.maximum(t - w // 2, 0), np.minimum(t + w // 2 - 1, n - 1)
        m = (t[None, :] >= lo[:, None]) & (t[None, :] <= hi[:, None])
        return m / (hi - lo + 1)[:, None]

    pool = np.zeros((4, 128, 4, 256), f)
    for g, w in enumerate((2, 4, 8, 16)):
        grid = np.kron(mean(4, w), mean(64, w)) - np.eye(256)
        line = mean(256, w) - np.eye(256)
        for n, m in enumerate((grid, line)):
            pool[g, :, 2 * n:2 * n + 2, :] = m.T.reshape(2, 128, 256).transpose(1, 0, 2)
    return {"bias": bias, "cst": cst, "hgm": hgm, "poolm": pool.reshape(4, 128, 1024)}


def kernel(**inputs):
    import concourse.bacc as bacc
    from concourse.bass_utils import run_bass_kernel_spmd as run

    a = {n: np.asarray(v) for n, v in inputs.items()}

    def col(v):
        v = v.reshape(-1, 128) if v.ndim == 1 else v.reshape(v.shape[0] * (v.shape[1] // 128), 128)
        return v.T

    lb = a["lb_logits_2"].reshape(2 * 3 * 16, 128).T
    cc = np.stack([a["c_2"][0].reshape(16, 128), a["c_ctx_2"].reshape(16, 128)], axis=1).reshape(32, 128).T
    parts = [col(a["g_mix_pre"][0]), col(a["g_mix_post"][0]), col(a["g_ffn_pre"][0]), col(a["g_ffn_post"][0]),
             col(a["pre_g_2"][0]), col(a["pre_g_2"][1]), col(a["post_g_2"][0]), col(a["post_g_2"][1]),
             col(a["ev_pool_scale_2"][0]), col(a["ev_conv_w_2"][0]), col(a["ev_conv_b_2"][0]),
             col(a["conv_w"][0]), col(a["conv_b"][0]), col(a["od_onorm_g_2"][0]), lb, col(a["ada_b_2"]), cc]
    arrays = {
        "xT": a["x"][0].T, "ctxT": a["ctx_2"][0].T, "pT": a["p"][0, 0].T,
        "vec": np.concatenate(parts, axis=1),
        "w_in": a["w_in"][0], "w_ba": a["w_branch_a"][0], "w_bb": a["w_branch_b"][0], "w_out": a["w_out"][0],
        "w_up": a["w_up"][0], "w_down": a["w_down"][0], "w_ple_in": a["w_ple_in"][0],
        "w_ple_gate": a["w_ple_gate"][0], "ada_w": a["ada_w_2"], "ev_w_in": a["ev_w_in_2"][0],
        "ev_pool_w": a["ev_pool_w_2"][0], "ev_w_out": a["ev_w_out_2"][0], "od_w_in": a["od_w_in_2"][0],
        "od_w_out": a["od_w_out_2"][0],
    }
    arrays.update(constants())
    arrays = {n: np.ascontiguousarray(v) for n, v in arrays.items()}
    nc = bacc.Bacc("TRN2", target_bir_lowering=False, num_devices=1)
    A = {n: nc.dram_tensor(f"in_{n}", v.shape, mybir.dt.from_np(v.dtype), kind="ExternalInput").ap()
         for n, v in arrays.items()}
    A["out"] = nc.dram_tensor("out_0", (D, T), F32, kind="ExternalOutput").ap()
    build(nc, A)
    r = run(nc, [{f"in_{n}": v for n, v in arrays.items()}], core_ids=[0])
    return r.results[0]["out_0"].T.reshape(1, T, D)
```
